# Optimizing a Trainium2 kernel written in Bass

```python
import math
import jax, jax.numpy as jnp
from jax import lax
import numpy as np

D_MODEL = 1024
BATCH = 1
SEQ = 512
DEPTH = 2

GRID_W = 64
CTX_LEN = 256
HEAD_DIM = 64
NA_HEADS = 4
NA_WIN_R = 8
NA_WIN_C = 16
ML_HEADS = 4
ML_CONV = 3
ML_CHUNK = 128
MLA_HEADS = 8
MLA_NOPE = 64
MLA_ROPE = 32
MLA_V = 64
Q_LORA = 384
KV_LORA = 256
NA_W = NA_HEADS * HEAD_DIM
ML_W = ML_HEADS * HEAD_DIM
MLA_W = MLA_HEADS * MLA_V
D_MIX = NA_W + ML_W + MLA_W
D_FF = -(-8 * D_MODEL // (3 * 256)) * 256
ROPE_BASE = 10000.0
EPS = 1e-6
Q_BLOCK = 128
NA_SCALE = HEAD_DIM ** -0.5
MLA_SCALE = (MLA_NOPE + MLA_ROPE) ** -0.5
IN_SPLITS = (NA_W, NA_W, NA_W, ML_W, ML_W, ML_W, ML_W, 4 * ML_HEADS, Q_LORA, KV_LORA, MLA_ROPE)
IN_OFFSETS = tuple(sum(IN_SPLITS[:i + 1]) for i in range(len(IN_SPLITS) - 1))
D_IN = sum(IN_SPLITS)

kernel_name = 'hybrid_na_mlstm_mla_dit_block'

def rms_norm(x, g):
    xf = x.astype(jnp.float32)
    y = xf * lax.rsqrt(jnp.mean(xf * xf, axis=-1, keepdims=True) + EPS)
    return (y * g).astype(x.dtype)

def modulation(cond, w_mod, b_mod):
    m = jax.nn.silu(cond) @ w_mod + b_mod
    return jnp.split(m, 6, axis=-1)

def modulate(x, g, shift, scale):
    return rms_norm(x, g) * (1.0 + scale[:, None, :]) + shift[:, None, :]

def swiglu(h, w_in, w_out):
    a, b = jnp.split(h @ w_in, 2, axis=-1)
    return (jax.nn.silu(a) * b) @ w_out

def flat_heads(a):
    return a.reshape(a.shape[0], a.shape[1], -1)

def axial_rope(n_tok, dim):
    n_freq = dim // 4
    inv = ROPE_BASE ** (-jnp.arange(n_freq, dtype=jnp.float32) / n_freq)
    t = jnp.arange(n_tok, dtype=jnp.int32)
    row = (t // GRID_W).astype(jnp.float32)
    col = (t % GRID_W).astype(jnp.float32)
    ang = jnp.concatenate([row[:, None] * inv, col[:, None] * inv], axis=-1)
    return jnp.cos(ang), jnp.sin(ang)

def apply_rope(x, cos, sin):
    half = x.shape[-1] // 2
    x1, x2 = x[..., :half], x[..., half:]
    cs = cos[:, None, :].astype(x.dtype)
    sn = sin[:, None, :].astype(x.dtype)
    return jnp.concatenate([x1 * cs - x2 * sn, x1 * sn + x2 * cs], axis=-1)

def attend(q, k, v, scale):
    s = jnp.einsum('bqhd,bkhd->bhqk', q, k).astype(jnp.float32) * scale
    p = jax.nn.softmax(s, axis=-1).astype(v.dtype)
    return jnp.einsum('bhqk,bkhd->bqhd', p, v)

def blocked_attention(q, k, v, scale):
    B, T, H, d = q.shape
    nb = T // Q_BLOCK
    qb = q.reshape(B, nb, Q_BLOCK, H, d).swapaxes(0, 1)
    ob = lax.map(lambda qi: attend(qi, k, v, scale), qb)
    return ob.swapaxes(0, 1).reshape(B, T, H, v.shape[-1])

def na_project(p, qk_gain):
    B, T, _ = p[0].shape
    q = rms_norm(p[0].reshape(B, T, NA_HEADS, HEAD_DIM), qk_gain[0])
    k = rms_norm(p[1].reshape(B, T, NA_HEADS, HEAD_DIM), qk_gain[1])
    v = p[2].reshape(B, T, NA_HEADS, HEAD_DIM)
    return q, k, v

def neighbourhood_attention(q, k, v, k_ctx, v_ctx, rpb):
    B, S, H, d = q.shape
    rows = S // GRID_W
    wr = min(NA_WIN_R, rows)
    qg, kg, vg = (a.reshape(B, rows, GRID_W, H, d) for a in (q, k, v))
    cols = np.arange(GRID_W)
    col_start = np.clip(cols - NA_WIN_C // 2, 0, GRID_W - NA_WIN_C)
    col_idx = col_start[:, None] + np.arange(NA_WIN_C)
    dc = col_idx - cols[:, None] + (NA_WIN_C - 1)
    n_loc = wr * NA_WIN_C

    def row_block(r):
        rs = jnp.clip(r - NA_WIN_R // 2, 0, rows - wr)
        q_r = lax.dynamic_index_in_dim(qg, r, axis=1, keepdims=False)
        k_w = lax.dynamic_slice_in_dim(kg, rs, wr, axis=1)[:, :, col_idx]
        v_w = lax.dynamic_slice_in_dim(vg, rs, wr, axis=1)[:, :, col_idx]
        dr = rs - r + jnp.arange(wr) + (NA_WIN_R - 1)
        bias = rpb[:, dr][:, :, dc].transpose(0, 2, 1, 3)
        s_loc = jnp.einsum('bchd,brcjhd->bhcrj', q_r, k_w).astype(jnp.float32) * NA_SCALE + bias
        s_ctx = jnp.einsum('bchd,bkhd->bhck', q_r, k_ctx).astype(jnp.float32) * NA_SCALE
        s = jnp.concatenate([s_loc.reshape(B, H, GRID_W, n_loc), s_ctx], axis=-1)
        p = jax.nn.softmax(s, axis=-1).astype(v.dtype)
        p_loc = p[..., :n_loc].reshape(B, H, GRID_W, wr, NA_WIN_C)
        p_ctx = p[..., n_loc:]
        return (jnp.einsum('bhcrj,brcjhd->bchd', p_loc, v_w)
                + jnp.einsum('bhck,bkhd->bchd', p_ctx, v_ctx))

    out = lax.map(row_block, jnp.arange(rows, dtype=jnp.int32))
    return out.swapaxes(0, 1).reshape(B, S, H, d)

def short_conv(x, w, b):
    K = w.shape[0]
    T = x.shape[1]
    xp = jnp.pad(x, ((0, 0), (K // 2, K - 1 - K // 2), (0, 0)))
    y = b + xp[:, 0:T] * w[0]
    for j in range(1, K):
        y = y + xp[:, j:j + T] * w[j]
    return jax.nn.silu(y)

def to_heads(a, H):
    B, T, _ = a.shape
    return a.reshape(B, T, H, -1).transpose(0, 2, 1, 3)

def mlstm_project(p, conv_w, conv_b, gate_b):
    qk = short_conv(jnp.concatenate([p[3], p[4]], axis=-1), conv_w, conv_b)
    q, k = jnp.split(qk, 2, axis=-1)
    q = to_heads(q, ML_HEADS).astype(jnp.float32)
    k = to_heads(k, ML_HEADS).astype(jnp.float32) * (HEAD_DIM ** -0.5)
    v = to_heads(p[5], ML_HEADS).astype(jnp.float32)
    gates = (p[7] + gate_b).astype(jnp.float32)
    return q, k, v, gates

def mlstm_chunkwise(q, k, v, log_i, log_f, state):
    B, H, T, d = q.shape
    L = ML_CHUNK
    nc = T // L

    def to_chunks(a):
        return jnp.moveaxis(a.reshape(B, H, nc, L, *a.shape[3:]), 2, 0)

    xs = (to_chunks(q), to_chunks(k), to_chunks(v), to_chunks(log_i), to_chunks(log_f))
    causal = np.tril(np.ones((L, L), dtype=bool))

    def step(carry, inp):
        C, n, m = carry
        qi, ki, vi, li, lf = inp
        b = jnp.cumsum(lf, axis=-1)
        g = b + m[..., None]
        D = jnp.where(causal, b[..., :, None] - b[..., None, :] + li[..., None, :], -jnp.inf)
        m_t = jnp.maximum(g, jnp.max(D, axis=-1))
        w_inter = jnp.exp(g - m_t)
        qk = jnp.einsum('bhtd,bhsd->bhts', qi, ki) * jnp.exp(D - m_t[..., None])
        num = (w_inter[..., None] * jnp.einsum('bhvk,bhtk->bhtv', C, qi)
               + jnp.einsum('bhts,bhsv->bhtv', qk, vi))
        den = w_inter * jnp.einsum('bhk,bhtk->bht', n, qi) + jnp.sum(qk, axis=-1)
        h = num / jnp.maximum(jnp.abs(den), jnp.exp(-m_t))[..., None]
        bL = b[..., -1]
        a = bL[..., None] - b + li
        m_new = jnp.maximum(bL + m, jnp.max(a, axis=-1))
        decay = jnp.exp(bL + m - m_new)
        wk = jnp.exp(a - m_new[..., None])
        C_new = decay[..., None, None] * C + jnp.einsum('bhs,bhsv,bhsk->bhvk', wk, vi, ki)
        n_new = decay[..., None] * n + jnp.einsum('bhs,bhsk->bhk', wk, ki)
        return (C_new, n_new, m_new), h

    state, hc = lax.scan(step, state, xs)
    return jnp.moveaxis(hc, 0, 2).reshape(B, H, T, d), state

def mlstm_bidir(q, k, v, gates, state_f, state_b):
    i_f, f_f, i_b, f_b = (g.transpose(0, 2, 1) for g in jnp.split(gates, 4, axis=-1))
    h_f, st_f = mlstm_chunkwise(q, k, v, i_f, jax.nn.log_sigmoid(f_f), state_f)
    flip = lambda a: jnp.flip(a, axis=2)
    h_b, st_b = mlstm_chunkwise(flip(q), flip(k), flip(v), flip(i_b), flip(jax.nn.log_sigmoid(f_b)), state_b)
    return h_f + flip(h_b), st_f, st_b

def mlstm_output(h, o, head_gain):
    B, H, T, d = h.shape
    hn = rms_norm(h.transpose(0, 2, 1, 3), head_gain)
    out = hn * jax.nn.sigmoid(o.reshape(B, T, H, d).astype(jnp.float32))
    return out.reshape(B, T, H * d).astype(o.dtype)

def mla_project(p, gq, gkv, w_uq, w_ukv, qk_gain, rope):
    B, T, _ = p[8].shape
    q = (rms_norm(p[8], gq) @ w_uq).reshape(B, T, MLA_HEADS, MLA_NOPE + MLA_ROPE)
    kv = (rms_norm(p[9], gkv) @ w_ukv).reshape(B, T, MLA_HEADS, MLA_NOPE + MLA_V)
    k_nope, v = kv[..., :MLA_NOPE], kv[..., MLA_NOPE:]
    k_rope = jnp.broadcast_to(p[10][:, :, None, :], (B, T, MLA_HEADS, MLA_ROPE))
    q = rms_norm(q, qk_gain[0])
    k = rms_norm(jnp.concatenate([k_nope, k_rope], axis=-1), qk_gain[1])
    if rope is not None:
        cos, sin = rope
        q = jnp.concatenate([q[..., :MLA_NOPE], apply_rope(q[..., MLA_NOPE:], cos, sin)], axis=-1)
        k = jnp.concatenate([k[..., :MLA_NOPE], apply_rope(k[..., MLA_NOPE:], cos, sin)], axis=-1)
    return q, k, v

def setup_inputs(seed: int = 0) -> dict:
    key = jax.random.key(seed)
    ks = jax.random.split(key, 24)
    D = D_MODEL

    def nrm(k, shape, s):
        return jax.random.normal(k, shape, jnp.float32) * s

    lin = jnp.linspace(3.0, 6.0, ML_HEADS, dtype=jnp.float32)
    zer = jnp.zeros((ML_HEADS,), jnp.float32)
    gate_base = jnp.concatenate([zer, lin, zer, lin])[None, :]
    return {
        'x': nrm(ks[0], (BATCH, SEQ, D), 1.0),
        'c': nrm(ks[1], (BATCH, D), 1.0),
        'ctx': nrm(ks[2], (BATCH, CTX_LEN, D), 1.0),
        'c_ctx': nrm(ks[3], (D,), 1.0),
        'w_mod': nrm(ks[4], (DEPTH, D, 6 * D), 0.5 * D ** -0.5),
        'b_mod': nrm(ks[5], (DEPTH, 6 * D), 0.02),
        'g_mix': 1.0 + nrm(ks[6], (DEPTH, D), 0.05),
        'g_ffn': 1.0 + nrm(ks[7], (DEPTH, D), 0.05),
        'w_in': nrm(ks[8], (DEPTH, D, D_IN), D ** -0.5),
        'b_gate': gate_base + nrm(ks[9], (DEPTH, 4 * ML_HEADS), 0.1),
        'na_qk_gain': 1.0 + nrm(ks[10], (DEPTH, 2, HEAD_DIM), 0.05),
        'na_rpb': nrm(ks[11], (DEPTH, NA_HEADS, 2 * NA_WIN_R - 1, 2 * NA_WIN_C - 1), 0.2),
        'ml_conv_w': nrm(ks[12], (DEPTH, ML_CONV, 2 * ML_W), ML_CONV ** -0.5),
        'ml_conv_b': nrm(ks[13], (DEPTH, 2 * ML_W), 0.02),
        'ml_head_gain': 1.0 + nrm(ks[14], (DEPTH, ML_HEADS, HEAD_DIM), 0.05),
        'mla_gq': 1.0 + nrm(ks[15], (DEPTH, Q_LORA), 0.05),
        'mla_gkv': 1.0 + nrm(ks[16], (DEPTH, KV_LORA), 0.05),
        'w_uq': nrm(ks[17], (DEPTH, Q_LORA, MLA_HEADS * (MLA_NOPE + MLA_ROPE)), Q_LORA ** -0.5),
        'w_ukv': nrm(ks[18], (DEPTH, KV_LORA, MLA_HEADS * (MLA_NOPE + MLA_V)), KV_LORA ** -0.5),
        'mla_qk_gain': 1.0 + nrm(ks[19], (DEPTH, 2, MLA_NOPE + MLA_ROPE), 0.05),
        'w_out': nrm(ks[20], (DEPTH, D_MIX, D), D_MIX ** -0.5),
        'w_ffn_in': nrm(ks[21], (DEPTH, D, 2 * D_FF), D ** -0.5),
        'w_ffn_out': nrm(ks[22], (DEPTH, D_FF, D), D_FF ** -0.5),
    }

def reference(x, c, ctx, c_ctx, w_mod, b_mod, g_mix, g_ffn, w_in, b_gate, na_qk_gain, na_rpb,
              ml_conv_w, ml_conv_b, ml_head_gain, mla_gq, mla_gkv, w_uq, w_ukv, mla_qk_gain,
              w_out, w_ffn_in, w_ffn_out):
    B, S, _ = x.shape
    rope = axial_rope(S, MLA_ROPE)
    zero_state = (jnp.zeros((B, ML_HEADS, HEAD_DIM, HEAD_DIM), jnp.float32),
                  jnp.zeros((B, ML_HEADS, HEAD_DIM), jnp.float32),
                  jnp.zeros((B, ML_HEADS), jnp.float32))
    xl, xc = x, ctx
    for l in range(DEPTH):
        need_ctx = l < DEPTH - 1
        sh1, sc1, gt1, sh2, sc2, gt2 = modulation(c, w_mod[l], b_mod[l])
        csh1, csc1, cgt1, csh2, csc2, cgt2 = modulation(c_ctx[None, :], w_mod[l], b_mod[l])
        pl = jnp.split(modulate(xl, g_mix[l], sh1, sc1) @ w_in[l], IN_OFFSETS, axis=-1)
        pc = jnp.split(modulate(xc, g_mix[l], csh1, csc1) @ w_in[l], IN_OFFSETS, axis=-1)

        qa_l, ka_l, va_l = na_project(pl, na_qk_gain[l])
        qa_c, ka_c, va_c = na_project(pc, na_qk_gain[l])
        oa_l = neighbourhood_attention(qa_l, ka_l, va_l, ka_c, va_c, na_rpb[l])

        qb_c, kb_c, vb_c, gb_c = mlstm_project(pc, ml_conv_w[l], ml_conv_b[l], b_gate[l])
        qb_l, kb_l, vb_l, gb_l = mlstm_project(pl, ml_conv_w[l], ml_conv_b[l], b_gate[l])
        hb_c, st_f, st_b = mlstm_bidir(qb_c, kb_c, vb_c, gb_c, zero_state, zero_state)
        hb_l, _, _ = mlstm_bidir(qb_l, kb_l, vb_l, gb_l, st_f, st_b)
        ob_l = mlstm_output(hb_l, pl[6], ml_head_gain[l])

        qc_l, kc_l, vc_l = mla_project(pl, mla_gq[l], mla_gkv[l], w_uq[l], w_ukv[l], mla_qk_gain[l], rope)
        qc_c, kc_c, vc_c = mla_project(pc, mla_gq[l], mla_gkv[l], w_uq[l], w_ukv[l], mla_qk_gain[l], None)
        oc_l = blocked_attention(qc_l, jnp.concatenate([kc_l, kc_c], axis=1),
                                 jnp.concatenate([vc_l, vc_c], axis=1), MLA_SCALE)

        mix_l = jnp.concatenate([flat_heads(oa_l), ob_l, flat_heads(oc_l)], axis=-1) @ w_out[l]
        xl = xl + gt1[:, None, :] * mix_l
        xl = xl + gt2[:, None, :] * swiglu(modulate(xl, g_ffn[l], sh2, sc2), w_ffn_in[l], w_ffn_out[l])

        if need_ctx:
            oa_c = attend(qa_c, ka_c, va_c, NA_SCALE)
            ob_c = mlstm_output(hb_c, pc[6], ml_head_gain[l])
            oc_c = attend(qc_c, kc_c, vc_c, MLA_SCALE)
            mix_c = jnp.concatenate([flat_heads(oa_c), ob_c, flat_heads(oc_c)], axis=-1) @ w_out[l]
            xc = xc + cgt1[:, None, :] * mix_c
            xc = xc + cgt2[:, None, :] * swiglu(modulate(xc, g_ffn[l], csh2, csc2), w_ffn_in[l], w_ffn_out[l])
    return xl


_drawn_inputs = setup_inputs


def setup_inputs(seed=0):
    import zlib

    import numpy as np

    out = dict(_drawn_inputs(seed))
    spreads = {}
    factors = {'g_mix': 6.633,
     'na_qk_gain': 8.0,
     'na_rpb': 8.0,
     'ml_conv_b': 36.826,
     'ml_head_gain': 8.0,
     'mla_gq': 8.0,
     'mla_gkv': 8.0,
     'mla_qk_gain': 8.0}
    for name, (base, spread) in spreads.items():
        noise = np.random.default_rng([zlib.crc32(name.encode()), seed]).standard_normal(out[name].shape)
        drawn = base * np.exp(spread * noise) if base else spread * noise
        out[name] = __import__('jax').numpy.asarray(drawn.astype(out[name].dtype))
    for name, factor in factors.items():
        out[name] = (out[name] * factor).astype(out[name].dtype)
    return out
```

```python
import concourse.bass as bass
from concourse import mybir
from contextlib import ExitStack
import numpy as np

D_MODEL, SEQ, CTX_LEN, DEPTH = 1024, 512, 256, 2
TOK = CTX_LEN + SEQ
GRID_W, HEAD_DIM = 64, 64
NA_HEADS, NA_WIN_R, NA_WIN_C = 4, 8, 16
ML_HEADS, ML_CHUNK = 4, 128
MLA_HEADS, NOPE, ROPE, V_DIM = 8, 64, 32, 64
QK_DIM = NOPE + ROPE
Q_LORA, KV_LORA = 384, 256
D_FF = -(-8 * D_MODEL // (3 * 256)) * 256
GRID_R = SEQ // GRID_W
EPS, ROPE_BASE = 1e-6, 10000.0
P = 128
KT = D_MODEL // P
TT = TOK // P
CT = CTX_LEN // P
NG = 4 * ML_HEADS
NDR = 2 * NA_WIN_R - 1
NDC = 2 * NA_WIN_C - 1
NEG = -1.0e30

UW = 1024
NA_V, NA_QK, NA_OUT = 0, 2, 6
ML_G, ML_QK, ML_O, ML_V, ML_OUT = 8, 9, 13, 15, 17
MA_CQ, MA_CKV, MA_KR, MA_V, MA_HEAD, MA_OUT = 19, 22, 24, 25, 26, 30
FF0 = 34
FF_GROUPS = (8, 8, 6)
assert sum(FF_GROUPS) * P == D_FF
FF_IN, FF_OUT = [], []
_u = FF0
for _n in FF_GROUPS:
    FF_IN.append(_u)
    FF_OUT.append(_u + 2 * _n)
    _u += 2 * _n + KT
UNITS = _u
RAW = 4
MODU = 12

C_GMIX, C_GFFN, C_BMOD = 0, 8, 16
C_NAQ, C_NAK = 64, 66
C_GI, C_GF, C_GM = 67, 68, 69
C_CONV = 70
C_HG = 86
C_CQ, C_CKV = 88, 91
C_MQ, C_MK = 93, 94
NCOL = 95


def psum_pair(ps, n):
    return ps[:, 1024 * n + 256:1024 * n + 1024]


def build(nc, x_t, c_t, w_mod, w_stream, cols, rpb, c_f32, c_rope, c_gate, c_dir, out):
    fp32, fp32r, bf16 = mybir.dt.float32, mybir.dt.float32r, mybir.dt.bfloat16
    ALU, ACT, AX = mybir.AluOpType, mybir.ActivationFunctionType, mybir.AxisListType
    es = ExitStack()
    with es:
        def sb(name, shape, dt=fp32, stack=es):
            return stack.enter_context(nc.sbuf_tensor(name, shape, dt))

        def sem(name):
            return es.enter_context(nc.semaphore(name))

        xres = sb("xres", [P, KT, TOK])
        hhi = sb("hhi", [P, KT, TOK], fp32r)
        hlo = sb("hlo", [P, KT, TOK], fp32r)
        raw = sb("raw", [P, RAW, UW])
        whi = sb("whi", [P, 2, UW], fp32r)
        wlo = sb("wlo", [P, 2, UW], fp32r)
        consts = sb("consts", [P, 3 * P + 256 + 64])
        dirm = sb("dirm", [P, 2 * P])
        ident = consts[:, 0:P]
        ones = consts[:, P:2 * P]
        ones2 = consts[:, 2 * P:3 * P]
        band = consts[:, 3 * P:3 * P + 256]
        colmask = consts[:, 3 * P + 256:3 * P + 320]
        identb = sb("identb", [P, P], bf16)
        dirmask = sb("dirmask", [P, 2, P], bf16)
        lc = sb("lc", [P, DEPTH, NCOL])
        mods = sb("mods", [P, DEPTH, 48, 2])
        amix = sb("amix", [P, DEPTH, 2, KT, 2])
        csil = sb("csil", [P, KT, 2])
        eps = sb("eps", [P, 1])
        stat = sb("stat", [P, 2, 8])
        psum = es.enter_context(nc.psum_tensor("psum", [P, 8 * 512], fp32))

        def bank(n):
            return psum[:, 512 * n:512 * n + 512]

        def scope(fn):
            with ExitStack() as s:
                d=fn(lambda name, shape, dt=fp32: sb(name, shape, dt, s)); return d

        def mod_scope(a):
            return dict(wm=a("wm", [P, 3, KT * 512]), row=a("modrow", [2, 48 * P]))

        def norm_scope(a):
            return dict(sq=a("n_sq", [P, 2, TOK]), r=a("n_r", [P, TOK]), t=a("n_t", [P, 2, TOK]))

        def na_scope(a):
            d = dict(qhi=a("naqhi", [P, 2, TOK], fp32r), qlo=a("naqlo", [P, 2, TOK], fp32r),
                     khi=a("nakhi", [P, TOK], fp32r), klo=a("naklo", [P, TOK], fp32r),
                     vhi=a("navhi", [P, TT, 256], fp32r), vlo=a("navlo", [P, TT, 256], fp32r),
                     bias=a("nabias", [P, NA_HEADS, 16, GRID_W]),
                     ohi=a("naohi", [P, 2, TOK], fp32r), olo=a("naolo", [P, 2, TOK], fp32r),
                     rb=a("narpb", [P, 4 * NA_HEADS * NDR]))
            pt = a("napthi", [P, 1, TT, 256], fp32r)
            d.update(p=a("nap", [P, 2, TOK]), pthi=pt, ptlo=a("naptlo", [P, 1, TT, 256], fp32r))
            d.update(s2=a("nas2", [P, 2, 512]), sq=a("nasq", [P, TOK]), r=a("nar", [P, TOK]), t=a("nat", [P, TOK]))
            return d

        def ml_scope(a):
            d = dict(qk=a("mlqk", [P, 4, TOK]), osig=a("mlosig", [P, 2, TOK]),
                        va=a("mlva", [P, TT, ML_HEADS, 65]), kt=a("mlkt", [P, TT, 256]),
                        tm=a("mltm", [P, TT, 4, 36]),
                        e=a("mle", [P, 2, TOK]), hin=a("mlhin", [P, 8, TT, 65]),
                        kw=a("mlkw", [P, 2, 2, 256]), st=a("mlst", [P, 2, 4, 130]),
                        small=a("mlsmall", [36, 6, 6]), dec=a("mldec", [P, 4, 6]),
                        hs=a("mlhs", [P, 2, 4, 65]), um=a("mlum", [P, 2, 130]), sel=a("mlsel", [36, 8 * P + 4 * P]),
                        blk=a("mlblk", [P, 130]),
                        den=a("mlden", [P, 8, TT]), mask=a("mlmask", [36, TOK]), ssq=a("mlssq", [P, ML_HEADS, TT]))
            with ExitStack() as s:
                d["rows"] = sb("mlrows", [36, 6, TOK], fp32, s)
            d.update(ohi=a("mlohi", [P, 2, TOK], fp32r), olo=a("mlolo", [P, 2, TOK], fp32r))
            return d

        def ma_scope(a):
            return dict(cqhi=a("cqhi", [P, 3, TOK], fp32r), cqlo=a("cqlo", [P, 3, TOK], fp32r),
                        ckhi=a("ckhi", [P, 2, TOK], fp32r), cklo=a("cklo", [P, 2, TOK], fp32r),
                        kr=a("krraw", [P, TOK]), sqk=a("masqk", [P, TOK]), sqq=a("masqq", [P, TOK]),
                        qhi=a("maqhi", [P, 1, TOK], fp32r), qlo=a("maqlo", [P, 1, TOK], fp32r),
                        khi=a("makhi", [P, TOK], fp32r), klo=a("maklo", [P, TOK], fp32r),
                        t=a("mat", [P, TOK]), t2=a("mat2", [P, TOK]), r=a("mar", [P, 2, TOK]),
                        rope=a("marope", [P, 2, SEQ]),
                        p=a("map", [P, 2, TOK]), pthi=a("mapthi", [P, 1, TT, 256], fp32r),
                        ptlo=a("maptlo", [P, 1, TT, 256], fp32r))

        def ff_scope(a):
            return dict(uhi=a("uhi", [P, 8, TOK], fp32r), ulo=a("ulo", [P, 8, TOK], fp32r),
                        sa=a("ffsa", [P, 2, TOK]), uf=a("ffuf", [P, 2, TOK]))

        MODS, NRM, NA, ML, MA, FF = (scope(f) for f in (mod_scope, norm_scope, na_scope, ml_scope, ma_scope, ff_scope))

        xin = sem("xin")
        mod_in = [sem(f"mod_in{i}") for i in range(3)]
        small_in = sem("small_in")
        raw_full = [sem(f"raw_full{i}") for i in range(RAW)]
        hi_done, lo_done = sem("hi_done"), sem("lo_done")
        w_used = sem("w_used")
        pe_phase, act_phase, dve_phase = sem("pe_phase"), sem("act_phase"), sem("dve_phase")
        act_chain, dve_chain = sem("act_chain"), sem("dve_chain")
        mod_ps, mod_row, mod_tr = sem("mod_ps"), sem("mod_row"), sem("mod_tr")
        sq_done, sq_used, st_done = sem("sq_done"), sem("sq_used"), sem("st_done")
        r_done, t_done, h_hi, h_lo = sem("r_done"), sem("t_done"), sem("h_hi"), sem("h_lo")
        s_ps, s_nmx, s_exp, s_rs, s_p = (sem(x) for x in ("scores", "negmax", "exps", "rsum", "probs"))
        t_ps, pt_hi, pt_lo = sem("probsT"), sem("probsT_hi"), sem("probsT_lo")
        pv_ps, o_hi, o_lo = sem("pv"), sem("o_hi"), sem("o_lo")
        x_free = sem("x_free")
        ff_free = sem("ff_free")
        ff_sa, ff_uf, ff_uhi = sem("ff_silu"), sem("ff_prod"), sem("ff_uhi")
        ev_ps, ev_a, ev_d = sem("ev_ps"), sem("ev_a"), sem("ev_d")
        out_done = sem("out_done")
        sq2, rs2 = sem("head_squares"), sem("head_rsqrt")
        bias_ps, bias_ev, o_ps = sem("bias_ps"), sem("bias_ev"), sem("o_ps")
        ml_t, ml_a, ml_d = sem("ml_tensor"), sem("ml_scalar"), sem("ml_vector")
        ma_t, ma_a, ma_d = sem("ma_tensor"), sem("ma_scalar"), sem("ma_vector")

        HG = D_FF // P
        XPL = 8 * (3 + len(FF_GROUPS))

        def u0(l, off):
            return l * UNITS + off

        def ranges(full):
            return [(CTX_LEN, TOK), (0, CTX_LEN)] if full else [(CTX_LEN, TOK)]

        def cls(r0):
            return 1 if r0 == 0 else 0

        def att_blocks(l):
            return ([0] if l < DEPTH - 1 else []) + [1, 2]

        def att_plan():
            plan, s, b = {}, 0, 0
            for l in range(DEPTH):
                for kind, heads in (("na", NA_HEADS), ("ma", MLA_HEADS)):
                    for h in range(heads):
                        steps = []
                        for blk in att_blocks(l):
                            for qt in (0, 1):
                                steps.append((s, b, blk, qt, CT if blk == 0 else TT))
                                s += 1
                            b += 1
                        plan[l, kind, h] = steps
            return plan

        PLAN = att_plan()
        NAJ = {(l, pr, j): 4 * l + 2 * pr + j for l in range(DEPTH) for pr in range(2) for j in range(2)}
        SMALLS = {(k, l): 16 * (5 * l + n) for l in range(DEPTH) for k, n in (("na", 1), ("ml", 4), ("ma", 5))}
        CHUNKS = (list(range(TT)), list(range(CT))[::-1] + list(range(CT, TT))[::-1])
        VHI = hhi[:, 4:8, :].rearrange("p k t -> p (k t)").rearrange("p (t n) -> p t n", t=TT)
        VLO = hlo[:, 4:8, :].rearrange("p k t -> p (k t)").rearrange("p (t n) -> p t n", t=TT)

        def OPS(l, part):
            return 16 * l + (0, 6, 12)[part] + 1

        def counts(names):
            at = {n: i + 1 for i, n in enumerate(names)}
            return lambda l, n: l * len(names) + at[n]

        T_ = counts(["tm", "dec", "kt0", "kt1", "kt2"]
                    + [f"{x}{r}" for r in range(8) for x in ("st", "cr", "in") if x != "st" or r % 2 == 0]
                    + [f"{x}{n}" for n in range(TT) for x in ("x", "u") if (n or x == "u") and (n < TT - 1 or x == "x")]
                    + ["ht"])
        A_ = counts(["sp"] + [f"cv{i}" for i in range(4)]
                    + ["o0", "o1", "v0", "v1", "v2", "ed", "tm", "dec", "kt0", "kt1", "kt2"]
                    + [f"{x}{r}" for r in range(8) for x in ("e", "h")] + ["sq", "rstd"])
        D_ = counts(["gates", "cv0", "rows", "cv1", "cv2", "cv3", "k8"] + [f"p{r}" for r in range(8)] + ["kw0"]
                    + [f"{x}{n + (x == 'kw')}" for n in range(TT) for x in ("kw", "s", "x")
                       if (x == "kw" and n < TT - 2) or (x == "s" and n < TT - 1) or (x == "x" and n)]
                    + ["hsum", "ssq", "hn", "out"])
        MT_ = counts([f"c{i}" for i in range(5)]
                     + [f"{x}{h}" for h in range(MLA_HEADS) for x in ("hk", "hq", "tk", "tq") if x != "hq" or h % 2 == 0])
        MA_A = counts(["s0", "s1", "s2", "r0", "s3", "s4", "r1", "kr"] + [f"v{t}" for t in range(TT)]
                      + [f"{x}{h}" for h in range(MLA_HEADS) for x in ("ak", "aq", "rk", "rq")])
        MD_ = counts(["cq", "ck"] + [f"{x}{h}" for h in range(MLA_HEADS) for x in ("dk", "dq")])

        block = es.enter_context(nc.Block())

        @block.sync
        def _(sp):
            for k in range(KT):
                sp.dma_start(xres[:, k, :], x_t[:, k, :]).then_inc(xin, 16)
            sp.dma_start(csil[:, :, :], c_t).then_inc(xin, 16)
            sp.dma_start(consts[:, :], c_f32).then_inc(xin, 16)
            sp.dma_start(dirm[:, :], c_dir).then_inc(xin, 16)
            sp.dma_start(lc[:, :, :], cols).then_inc(xin, 16)
            def load(u, slot):
                sp.dma_start(raw[:, slot, :], w_stream[bass.ds(u, 1), :, :].rearrange("o p w -> (o p) w"))\
                    .then_inc(raw_full[slot], 16)
            for s in range(RAW):
                load(s, s)
            with sp.Fori(1, DEPTH * UNITS // RAW) as i:
                for s in range(RAW):
                    sp.wait_ge(lo_done, i * RAW + (s + 1 - RAW))
                    load(i * RAW + s, s)
            sp.wait_ge(x_free, 2 + DEPTH * XPL)
            for k in range(KT):
                sp.dma_start(out[:, k, :], xres[:, k, CTX_LEN:TOK]).then_inc(out_done, 16)
            sp.wait_ge(out_done, 16 * KT)

        @block.gpsimd
        def _(pool):
            def lo(u, q, first=False):
                pool.wait_ge(hi_done, u + 1)
                if not first:
                    pool.wait_ge(w_used, u - 1)
                nc.gpsimd.tensor_tensor(wlo[:, q % 2, :], raw[:, q % RAW, :], whi[:, q % 2, :],
                                        ALU.subtract).then_inc(lo_done, 1)
            for q in range(RAW):
                lo(q, q, first=q < 2)
            with pool.Fori(1, DEPTH * UNITS // RAW) as i:
                for q in range(RAW):
                    lo(i * RAW + q, q)

        @block.scalar
        def _(act):
            A = nc.scalar.activation
            chain, hi_next, nph, smalls = [0], [0], [0], [0]

            def seq(ins):
                chain[0] += 1
                ins.then_inc(act_chain, 1)
                act.wait_ge(act_chain, chain[0])

            def hi(u, q, first=False):
                if isinstance(u, int):
                    act.wait_ge(raw_full[q % RAW], 16 * (u // RAW + 1))
                if not first:
                    act.wait_ge(w_used, u - 1)
                A(whi[:, q % 2, :], raw[:, q % RAW, :], ACT.Copy).then_inc(hi_done, 1)

            def his(upto):
                while hi_next[0] < min(upto, DEPTH * UNITS):
                    hi(hi_next[0], hi_next[0], first=hi_next[0] < 2)
                    hi_next[0] += 1

            def barrier(next_unit):
                his(next_unit + 2)
                nph[0] += 1
                act.drain().then_inc(act_phase, 1)
                act.wait_ge(pe_phase, nph[0])
                act.wait_ge(dve_phase, nph[0])

            def rsqrt_of(dst, src, scale):
                n = dst.shape[0]
                seq(A(dst, src, ACT.Ln, bias=eps[0:n, 0:1], scale=scale))
                return A(dst, dst, ACT.Exp, scale=-0.5)

            def small(dst, src):
                smalls[0] += 16
                act.dma_start(dst, src).then_inc(small_in, 16)

            def mod_phase(l):
                def load(n):
                    act.dma_start(MODS["wm"][:, n % 3, :].rearrange("p (k n) -> p k n", k=KT),
                                  w_mod[l, n]).then_inc(mod_in[n % 3], 16)
                if l == 0:
                    act.wait_ge(xin, 16 * (KT + 4))
                    seq(A(csil[:, :, :], csil[:, :, :], ACT.Silu))
                for n in range(3):
                    load(n)
                for n in range(MODU):
                    act.wait_ge(mod_ps, l * MODU + n + 1)
                    A(MODS["row"][:, 512 * n:512 * n + 512], bank(n % 2)[0:2, :], ACT.Copy).then_inc(mod_row, 1)
                    if n + 3 < MODU:
                        load(n + 3)
                act.wait_ge(mod_tr, l + 1)

            def norm_phase(l, which, full):
                n0 = 16 * l + 8 * which
                q0 = 0 if full else CTX_LEN
                for k in range(KT):
                    if k >= 2:
                        act.wait_ge(sq_used, 7 * (2 * l + which) + k - 1)
                    A(NRM["sq"][:, k % 2, q0:], xres[:, k, q0:], ACT.Square).then_inc(sq_done, 1)
                act.wait_ge(st_done, 2 * l + which + 1)
                rsqrt_of(NRM["r"][:, q0:], psum_pair(psum, 3)[:, q0:], 1.0 / D_MODEL).then_inc(r_done, 1)
                for k in range(KT):
                    act.wait_ge(t_done, n0 + k + 1)
                    rr = ranges(full)
                    for r0, r1 in rr:
                        ins = A(hhi[:, k, r0:r1], NRM["t"][:, k % 2, r0:r1], ACT.Identity,
                                bias=mods[:, l, 24 * which + k, cls(r0):cls(r0) + 1])
                    ins.then_inc(h_hi, 1)

            def na_inputs(l):
                small(NA["rb"][:, :], rpb[l])
                act.wait_ge(w_used, u0(l, NA_V) + 2)
                for b in range(3):
                    A(NA["vhi"][:, 2 * b:2 * b + 2, :], bank(b).rearrange("p (t n) -> p t n", t=2),
                      ACT.Copy).then_inc(ev_a, 1)

            def na_pair(l, pr):
                for j in (0, 1):
                    u = u0(l, NA_QK) + 2 * pr + j
                    act.wait_ge(w_used, u + 1)
                    his(u + 3)
                    n = NAJ[l, pr, j]
                    if j:
                        act.wait_ge(ev_ps, n)
                    A(NA["sq"][:, :], psum_pair(psum, 2 + j), ACT.Square).then_inc(sq2, 1)
                    act.wait_ge(ev_ps, n + 1)
                    if j:
                        act.wait_ge(ev_d, n)
                    rsqrt_of(NA["r"][:, :], psum_pair(psum, j), 1.0 / HEAD_DIM).then_inc(rs2, 1)

            def att_act(S, l, kind, h, scale, rows):
                steps = PLAN[l, kind, h]
                last = steps[-1][0]

                def exp_of(s, b, blk, qt, nk):
                    act.wait_ge(s_nmx, s + 1)
                    if s >= 2:
                        act.wait_ge(t_ps, s - 1)
                    sc = psum_pair(psum, s % 2)
                    st = stat[:, s % 2, :]
                    pb = S["p"][:, s % 2, :]
                    if kind == "na" and blk:
                        A(pb[:, 0:CTX_LEN], sc[:, 0:CTX_LEN], ACT.Exp, bias=st[:, 2:3], accum_out=st[:, 4:5])
                        A(pb[:, CTX_LEN:], S["s2"][:, s % 2, :], ACT.Exp, bias=st[:, 2:3],
                          accum_out=st[:, 5:6]).then_inc(s_exp, 1)
                    else:
                        A(pb[:, 0:nk * P], sc[:, 0:nk * P], ACT.Exp, bias=st[:, 2:3], scale=scale,
                          accum_out=st[:, 4:5]).then_inc(s_exp, 1)

                def norm_of(s, b, blk, qt, nk):
                    act.wait_ge(s_rs, s + 1)
                    pb = S["p"][:, s % 2, 0:nk * P]
                    A(pb, pb, ACT.Copy, scale=stat[:, s % 2, 6:7]).then_inc(s_p, 1)

                def hi_of(s, b, blk, qt, nk):
                    act.wait_ge(t_ps, s + 1)
                    if b >= 1:
                        act.wait_ge(pv_ps, b)
                    A(S["pthi"][:, 0, 0:nk, P * qt:P * qt + P],
                      psum_pair(psum, 2)[:, 0:nk * P].rearrange("p (k q) -> p k q", q=P),
                      ACT.Copy).then_inc(pt_hi, 1)

                for n, st in enumerate(steps):
                    exp_of(*st)
                    if n:
                        hi_of(*steps[n - 1])
                    norm_of(*st)
                hi_of(*steps[-1])

            def ml_act(l, full):
                rows, tm, e, va = ML["rows"], ML["tm"], ML["e"], ML["va"]
                small(ML["sel"][:, :], c_gate[:, 0:12 * P])
                small(ML["mask"][:, :], c_gate[:, 12 * P:12 * P + TOK])
                small(ML["blk"][:, :], c_rope[:, 2 * SEQ:2 * SEQ + 130])
                his(u0(l, ML_G) + 3)
                act.wait_ge(ml_d, D_(l, "gates"))
                seq(A(rows[:, 2, :], rows[:, 1, :], ACT.Abs))
                seq(A(rows[:, 2, :], rows[:, 2, :], ACT.Exp, scale=-1.0))
                A(rows[:, 2, :], rows[:, 2, :], ACT.Ln, bias=1.0).then_inc(ml_a, 1)
                for i in range(4):
                    his(u0(l, ML_QK) + i + 3)
                    act.wait_ge(ml_d, D_(l, f"cv{i}"))
                    A(ML["qk"][:, i, :], ML["qk"][:, i, :], ACT.Silu).then_inc(ml_a, 1)
                for i in range(2):
                    u = u0(l, ML_O) + i
                    his(u + 3)
                    act.wait_ge(w_used, u + 1)
                    A(ML["osig"][:, i, :], psum_pair(psum, 1 + i), ACT.Sigmoid).then_inc(ml_a, 1)
                his(u0(l, ML_V) + 2)
                act.wait_ge(w_used, u0(l, ML_V) + 2)
                for i in range(3):
                    A(va[:, 2 * i:2 * i + 2, :, 0:64],
                      bank((6, 7, 0)[i]).rearrange("p (t h d) -> p t h d", t=2, h=4), ACT.Copy).then_inc(ml_a, 1)
                his(u0(l, ML_V) + 4)
                act.wait_ge(ml_d, D_(l, "rows"))
                A(ML["small"][:, 3, :], ML["small"][:, 2, :], ACT.Exp).then_inc(ml_a, 1)
                act.wait_ge(ml_t, T_(l, "tm"))
                for g in range(2):
                    v = bank(4 + g)[:, 0:432].rearrange("p (c q r) -> p c q r", c=3, q=4)
                    A(tm[:, 3 * g:3 * g + 3, 0, :], v[:, :, 0, :], ACT.Copy)
                    ins = A(tm[:, 3 * g:3 * g + 3, 1:4, :], v[:, :, 1:4, :], ACT.Exp)
                ins.then_inc(ml_a, 1)
                act.wait_ge(ml_t, T_(l, "dec"))
                A(ML["dec"][:, :, :], bank(1)[:, 0:24].rearrange("p (x c) -> p x c", x=4), ACT.Copy).then_inc(ml_a, 1)
                for i in range(3):
                    act.wait_ge(ml_t, T_(l, f"kt{i}"))
                    A(ML["kt"][:, 2 * i:2 * i + 2, :], bank((6, 7, 0)[i]).rearrange("p (t n) -> p t n", t=2),
                      ACT.Copy).then_inc(ml_a, 1)
                for r in range(8):
                    h, d = r // 2, r % 2
                    act.wait_ge(ml_t, T_(l, f"cr{r}"))
                    if r >= 2:
                        act.wait_ge(ml_t, T_(l, f"in{r - 2}"))
                    elif r == 0:
                        act.wait_ge(ml_a, A_(l, "tm"))
                    for c in range(TT):
                        ins = A(e[:, d, P * c:P * c + P], psum_pair(psum, 1)[:, P * c:P * c + P], ACT.Exp,
                                bias=tm[:, c, 0, 32 * d + h:32 * d + h + 1])
                    ins.then_inc(ml_a, 1)
                    act.wait_ge(ml_t, T_(l, f"in{r}"))
                    for g in range(2):
                        ins = A(ML["hin"][:, 4 * d + h, 3 * g:3 * g + 3, :],
                                bank(4 + 2 * d + g)[:, 0:390].rearrange("p (c n) -> p c n", c=3)
                                [:, :, 65 * (h % 2):65 * (h % 2) + 65], ACT.Copy)
                    ins.then_inc(ml_a, 1)
                act.wait_ge(ml_d, D_(l, "hsum"))
                sq = e[:, :, :].rearrange("p a t -> p (a t)").rearrange("p (h c n) -> p h c n", h=4, c=TT)
                A(sq, ML["hin"][:, 0:4, :, 0:64], ACT.Square).then_inc(ml_a, 1)
                act.wait_ge(ml_d, D_(l, "ssq"))
                rsqrt_of(ML["ssq"][:, :, :], ML["ssq"][:, :, :], 1.0 / HEAD_DIM).then_inc(ml_a, 1)

            def ma_act(l, full):
                q0 = 0 if full else CTX_LEN
                small(MA["rope"][:, :, :], c_rope[:, 0:2 * SEQ].rearrange("p (a t) -> p a t", a=2))
                for n, (off, cnt, div) in enumerate(((MA_CQ, 3, Q_LORA), (MA_CKV, 2, KV_LORA))):
                    for i in range(cnt):
                        u = u0(l, off) + i
                        his(u + 3)
                        act.wait_ge(w_used, u + 1)
                        if n or i:
                            act.wait_ge(ma_t, MT_(l, "c%d" % (3 * n + i - 1)))
                        A(MA["sqq"][:, :], psum_pair(psum, i), ACT.Square).then_inc(ma_a, 1)
                    act.wait_ge(ma_t, MT_(l, "c%d" % (3 * n + cnt - 1)))
                    rsqrt_of(MA["r"][:, n, :], psum_pair(psum, 3), 1.0 / div).then_inc(ma_a, 1)
                u = u0(l, MA_KR)
                his(u + 3)
                act.wait_ge(w_used, u + 1)
                seq(A(MA["kr"][64:128, :], psum_pair(psum, 2)[64:128, :], ACT.Copy))
                A(MA["sqk"][64:96, :], MA["kr"][64:96, :], ACT.Square).then_inc(ma_a, 1)
                his(u + 4)
                act.wait_ge(w_used, u + 2)
                for t in range(TT):
                    A(VHI[:, t, :], bank(t), ACT.Copy).then_inc(ma_a, 1)

            def ma_head_act(l, h, full):
                q0 = 0 if full else CTX_LEN
                u = u0(l, MA_HEAD) + h // 2
                his(u + 2)
                act.wait_ge(ma_t, MT_(l, f"hk{h}"))
                A(MA["sqk"][0:64, :], psum_pair(psum, 1)[0:64, :], ACT.Square).then_inc(ma_a, 1)
                if h % 2 == 0:
                    act.wait_ge(ma_t, MT_(l, f"hq{h}"))
                else:
                    act.wait_ge(w_used, u + 1)
                A(MA["sqq"][0:96, q0:], psum_pair(psum, 0)[0:96, q0:], ACT.Square).then_inc(ma_a, 1)
                act.wait_ge(ma_t, MT_(l, f"tk{h}"))
                rsqrt_of(MA["r"][:, 1, :], psum_pair(psum, 3), 1.0 / QK_DIM).then_inc(ma_a, 1)
                act.wait_ge(ma_t, MT_(l, f"tq{h}"))
                rsqrt_of(MA["r"][:, 0, q0:], psum_pair(psum, 2)[:, q0:], 1.0 / QK_DIM).then_inc(ma_a, 1)

            def ff_act(l, full):
                q0 = 0 if full else CTX_LEN

                def silu(gj, par):
                    act.wait_ge(w_used, FFB(gj) + 2)
                    act.wait_ge(ff_free, gj + 1)
                    A(FF["sa"][:, par, q0:], psum_pair(psum, 2 * par)[:, q0:], ACT.Silu).then_inc(ff_sa, 1)

                j0 = 0
                for g, n in enumerate(FF_GROUPS):
                    b = u0(l, FF_IN[g])
                    gj = l * HG + j0
                    FFB = lambda x, b=b, gj=gj: b + 2 * (x - gj)
                    his(b + 4)
                    silu(gj, 0)
                    with act.Fori(1, n // 2) as i:
                        for jj in range(2):
                            for ab in range(2):
                                q = 2 * jj + ab
                                act.wait_ge(raw_full[(b + q) % RAW], i * 16 + 16 * ((b + q) // RAW + 1))
                                hi(i * 4 + (b + q), b + q)
                            if jj == 0:
                                silu(i * 2 + (gj - 1), 1)
                            else:
                                silu(i * 2 + gj, 0)
                    hi_next[0] = b + 2 * n
                    his(b + 2 * n + 2)
                    silu(gj + n - 1, 1)
                    his(u0(l, FF_OUT[g]) + KT + (2 if g < len(FF_GROUPS) - 1 else 0))
                    j0 += n

            for l in range(DEPTH):
                full = l < DEPTH - 1
                mod_phase(l)
                barrier(u0(l, 0))
                norm_phase(l, 0, True)
                barrier(u0(l, 0))
                na_inputs(l)
                barrier(u0(l, NA_QK))
                for pr in range(2):
                    na_pair(l, pr)
                    barrier(u0(l, NA_QK) + 2 * pr + 2)
                    for a in range(2):
                        att_act(NA, l, "na", 2 * pr + a, 1.0, None)
                    barrier(u0(l, NA_QK) + 2 * pr + 2)
                his(u0(l, ML_G))
                barrier(u0(l, ML_G))
                ml_act(l, full)
                his(u0(l, MA_CQ))
                barrier(u0(l, MA_CQ))
                ma_act(l, full)
                barrier(u0(l, MA_HEAD))
                for h in range(MLA_HEADS):
                    ma_head_act(l, h, full)
                    barrier(u0(l, MA_HEAD) + (h + 1) // 2)
                    att_act(MA, l, "ma", h, QK_DIM ** -0.5, None)
                    barrier(u0(l, MA_HEAD) + (h + 1) // 2)
                his(u0(l, FF0))
                barrier(u0(l, FF0))
                norm_phase(l, 1, full)
                barrier(u0(l, FF0))
                ff_act(l, full)
                barrier(u0(l + 1, 0))

        @block.tensor
        def _(pe):
            mm = nc.tensor.matmul
            nph = [0]

            def barrier():
                nph[0] += 1
                pe.drain().then_inc(pe_phase, 1)
                pe.wait_ge(act_phase, nph[0])
                pe.wait_ge(dve_phase, nph[0])

            def mm3(dst, ah, al, bh, bl, first, last):
                mm(dst, ah, bh, start=first, stop=False)
                mm(dst, ah, bl, start=False, stop=False)
                return mm(dst, al, bh, start=False, stop=last)

            def unit(u):
                pe.wait_ge(lo_done, u + 1)
                return whi[:, u % 2, :], wlo[:, u % 2, :]

            def feature_unit(u, pair, rr, srch=None, srcl=None, m=P, nk=KT, at=0, done=True):
                srch, srcl = (hhi, hlo) if srch is None else (srch, srcl)
                wh, wl = whi[:, u % 2, :], wlo[:, u % 2, :]
                for r0, r1 in rr:
                    dst = psum_pair(psum, pair)[0:m, r0:r1]
                    for k in range(nk):
                        c = at + k * m
                        ins = mm3(dst, wh[:, c:c + m], wl[:, c:c + m], srch[:, k, r0:r1], srcl[:, k, r0:r1],
                                  k == 0, k == nk - 1)
                if done:
                    ins.then_inc(w_used, 1)
                return ins

            def out_units(l, part, ubase, nk, oh, ol, rr):
                per = UW // (nk * P)
                for m in range(KT):
                    u = u0(l, ubase) + m // per
                    if m % per == 0:
                        unit(u)
                    g = l * XPL + part * KT + m
                    if g - 1 > 0:
                        pe.wait_ge(x_free, g - 1)
                    ins = feature_unit(u, m % 4, rr, oh, ol, nk=nk, at=(m % per) * nk * P, done=False)
                    ins.then_inc(w_used if m % per == per - 1 else o_ps, 1)

            def mod_phase(l):
                if l == 0:
                    pe.wait_ge(act_chain, 1)
                for n in range(MODU):
                    pe.wait_ge(mod_in[n % 3], 16 * ((l * MODU + n) // 3 + 1))
                    if n >= 2:
                        pe.wait_ge(mod_row, l * MODU + n - 1)
                    for k in range(KT):
                        ins = mm(bank(n % 2)[0:2, :], csil[:, k, :],
                                 MODS["wm"][:, n % 3, 512 * k:512 * k + 512], start=k == 0, stop=k == KT - 1)
                    ins.then_inc(mod_ps, 1)
                pe.wait_ge(mod_row, (l + 1) * MODU)
                pe.wait_ge(xin, 16 * (KT + 4))
                for j in range(48):
                    ins = nc.tensor.transpose(bank(2)[:, 2 * j:2 * j + 2], MODS["row"][0:2, P * j:P * j + P],
                                              ident[0:2, 0:2])
                ins.then_inc(mod_tr, 1)

            def norm_phase(l, which, full):
                n0 = 16 * l + 8 * which
                for k in range(KT):
                    pe.wait_ge(sq_done, n0 + k + 1)
                    for r0, r1 in ranges(full):
                        ins = mm(psum_pair(psum, 3)[:, r0:r1], ones, NRM["sq"][:, k % 2, r0:r1],
                                 start=k == 0, stop=k == KT - 1)
                    ins.then_inc(sq_used if k < KT - 1 else st_done, 1)

            def na_inputs(l):
                ua, ub = u0(l, NA_V), u0(l, NA_V) + 1
                (ah, al), (bh, bl) = unit(ua), unit(ub)
                for t in range(TT):
                    dst = bank(t // 2)[:, 256 * (t % 2):256 * (t % 2) + 256]
                    for k in range(KT):
                        wh, wl = (ah, al) if k < 4 else (bh, bl)
                        c = 256 * (k % 4)
                        mm(dst, hhi[:, k, P * t:P * t + P], wh[:, c:c + 256], start=k == 0, stop=False)
                        mm(dst, hlo[:, k, P * t:P * t + P], wh[:, c:c + 256], start=False, stop=False)
                        ins = mm(dst, hhi[:, k, P * t:P * t + P], wl[:, c:c + 256], start=False, stop=k == KT - 1)
                ins.then_inc(w_used, 2)
                pe.wait_ge(small_in, SMALLS["na", l])
                for g in range(16):
                    if g >= 4:
                        pe.wait_ge(bias_ev, 32 * l + 2 * (g - 3))
                    for half in (0, 64):
                        ins = mm(bank(4 + g % 4)[half:half + 64, 0:240], band[:, 60 - 4 * g:60 - 4 * g + 64],
                                 NA["rb"][:, :], start=True, stop=True)
                    ins.then_inc(bias_ps, 1)

            def na_pair(l, pr):
                for j in (0, 1):
                    u = u0(l, NA_QK) + 2 * pr + j
                    unit(u)
                    feature_unit(u, 2 + j, ranges(True))
                for j in (0, 1):
                    pe.wait_ge(sq2, NAJ[l, pr, j] + 1)
                    for r0, r1 in ranges(True):
                        ins = mm(psum_pair(psum, j)[:, r0:r1], ones2, NA["sq"][:, r0:r1], start=True, stop=True)
                    ins.then_inc(ev_ps, 1)

            def att_pe(S, l, kind, h, qh, ql, kh, kl, vt):
                steps = PLAN[l, kind, h]

                def scores(s, b, blk, qt, nk):
                    if s >= 2:
                        pe.wait_ge(s_exp, s - 1)
                    q0 = blk * 256 + qt * P
                    for r0, r1 in ([(0, CTX_LEN)] if blk == 0 else ranges(True)):
                        ins = mm3(psum_pair(psum, s % 2)[:, r0:r1], qh[:, q0:q0 + P], ql[:, q0:q0 + P],
                                  kh[:, r0:r1], kl[:, r0:r1], True, True)
                    ins.then_inc(s_ps, 1)

                def turn(s, b, blk, qt, nk):
                    pe.wait_ge(s_p, s + 1)
                    if s >= 1:
                        pe.wait_ge(pt_lo, s)
                    for k in range(nk):
                        ins = nc.tensor.transpose(psum_pair(psum, 2)[:, P * k:P * k + P],
                                                  S["p"][:, s % 2, P * k:P * k + P], ident)
                    ins.then_inc(t_ps, 1)

                def values(s, b, blk, qt, nk):
                    pe.wait_ge(pt_lo, s + 1)
                    if b >= 2:
                        pe.wait_ge(o_lo, b - 1)
                    for k in range(nk):
                        vh, vl = vt(k)
                        ins = mm3(bank(6 + b % 2)[:, 0:256], vh, vl, S["pthi"][:, 0, k, :], S["ptlo"][:, 0, k, :],
                                  k == 0, k == nk - 1)
                    ins.then_inc(pv_ps, 1)

                for n, st in enumerate(steps):
                    scores(*st)
                    if n:
                        turn(*steps[n - 1])
                    if n >= 2 and steps[n - 2][3] == 1:
                        values(*steps[n - 2])
                turn(*steps[-1])
                values(*steps[-1])

            def ml_pe(l, full):
                rows, tm, e, va, sel, qk = ML["rows"], ML["tm"], ML["e"], ML["va"], ML["sel"], ML["qk"]
                for i in range(7):
                    u = u0(l, ML_G) + i
                    unit(u)
                    if i == 4:
                        pe.wait_ge(ml_d, D_(l, "gates"))
                    elif i > 4:
                        pe.wait_ge(ml_d, D_(l, f"cv{i - 5}"))
                    feature_unit(u, i % 4, ranges(True))
                ua = u0(l, ML_V)
                (ah, al), (bh, bl) = unit(ua), unit(ua + 1)
                for t in range(TT):
                    if t % 2 == 0:
                        pe.wait_ge(ml_d, D_(l, "cv2" if t < 4 else "cv3"))
                    dst = bank((6, 7, 0)[t // 2])[:, 256 * (t % 2):256 * (t % 2) + 256]
                    for k in range(KT):
                        wh, wl = (ah, al) if k < 4 else (bh, bl)
                        c = 256 * (k % 4)
                        mm(dst, hhi[:, k, P * t:P * t + P], wh[:, c:c + 256], start=k == 0, stop=False)
                        mm(dst, hlo[:, k, P * t:P * t + P], wh[:, c:c + 256], start=False, stop=False)
                        ins = mm(dst, hhi[:, k, P * t:P * t + P], wl[:, c:c + 256], start=False, stop=k == KT - 1)
                ins.then_inc(w_used, 2)
                pe.wait_ge(ml_d, D_(l, "rows"))
                pe.wait_ge(ml_a, A_(l, "o1"))
                for c in range(TT):
                    for q, row in enumerate((0, 5, 4, 1)):
                        o = 144 * (c % 3) + 36 * q
                        ins = nc.tensor.transpose(bank(4 + c // 3)[:, o:o + 36], rows[:, row, P * c:P * c + P],
                                                  ident[0:36, 0:36])
                ins.then_inc(ml_t, 1)
                pe.wait_ge(ml_a, A_(l, "ed"))
                pe.wait_ge(small_in, SMALLS["ml", l])
                for x in range(4):
                    ins = mm(bank(1)[:, 6 * x:6 * x + 6], sel[:, 8 * P + P * x:9 * P + P * x], ML["small"][:, 3, :],
                             start=True, stop=True)
                ins.then_inc(ml_t, 1)
                pe.wait_ge(ml_d, D_(l, "k8"))
                for b in range(3):
                    pe.wait_ge(ml_a, A_(l, f"v{b}"))
                    for t in range(2):
                        for pr in range(2):
                            ins = nc.tensor.transpose(bank((6, 7, 0)[b])[:, 256 * t + P * pr:256 * t + P * pr + P],
                                                      qk[:, 2 + pr, P * (2 * b + t):P * (2 * b + t) + P], ident)
                    ins.then_inc(ml_t, 1)
                for r in range(8):
                    h, d = r // 2, r % 2
                    lo = 64 * (h % 2)
                    if d == 0:
                        pe.wait_ge(ml_a, A_(l, "kt2"))
                        if h:
                            pe.wait_ge(ml_d, D_(l, f"p{r - 1}"))
                        for c in range(TT):
                            s = slice(P * c, P * c + P)
                            ins = mm(psum_pair(psum, 0)[:, s], qk[lo:lo + 64, 2 + h // 2, s], qk[lo:lo + 64, h // 2, s],
                                     start=True, stop=True)
                        ins.then_inc(ml_t, 1)
                    if r:
                        pe.wait_ge(ml_a, A_(l, f"e{r - 1}"))
                    for r0, r1 in ranges(True):
                        dst = psum_pair(psum, 1)[:, r0:r1]
                        x = 4 * d + h
                        mm(dst, sel[:, P * x:P * x + P], rows[:, 2, r0:r1], start=True, stop=False)
                        ins = mm(dst, identb[:, :],
                                 dirmask[:, d, :].unsqueeze(1).broadcast_to([P, (r1 - r0) // P, P]),
                                 start=False, stop=True)
                    ins.then_inc(ml_t, 1)
                    pe.wait_ge(ml_d, D_(l, f"p{r}"))
                    if r >= 2:
                        pe.wait_ge(ml_a, A_(l, f"h{r - 2}"))
                    for c in range(TT):
                        ins = mm(bank(4 + 2 * d + c // 3)[:, 130 * (c % 3):130 * (c % 3) + 130],
                                 e[:, d, P * c:P * c + P],
                                 va[:, c, 2 * (h // 2):2 * (h // 2) + 2, :].rearrange("p h n -> p (h n)"),
                                 start=True, stop=True)
                    ins.then_inc(ml_t, 1)
                pe.wait_ge(ml_a, A_(l, "h7"))
                for n in range(TT):
                    if n:
                        pe.wait_ge(ml_d, D_(l, f"s{n - 1}"))
                        if n >= 3:
                            pe.wait_ge(ml_d, D_(l, f"x{n - 2}"))
                        for d in range(2):
                            c = CHUNKS[d][n]
                            for pr in range(2):
                                ins = mm(bank(2 * (n % 2) + d)[:, 130 * pr:130 * pr + 130],
                                         qk[:, pr, P * c:P * c + P], ML["st"][:, n % 2, 2 * d + pr, :],
                                         start=True, stop=True)
                        ins.then_inc(ml_t, 1)
                    if n < TT - 1:
                        pe.wait_ge(ml_d, D_(l, f"kw{n}"))
                        if n >= 2:
                            pe.wait_ge(ml_d, D_(l, f"s{n - 2}"))
                        for d in range(2):
                            c = CHUNKS[d][n]
                            for pr in range(2):
                                ins = mm(bank(4 + 2 * (n % 2) + d)[:, 130 * pr:130 * pr + 130],
                                         ML["kw"][:, n % 2, d, P * pr:P * pr + P],
                                         va[:, c, 2 * pr:2 * pr + 2, :].rearrange("p h n -> p (h n)"),
                                         start=True, stop=True)
                        ins.then_inc(ml_t, 1)
                pe.wait_ge(ml_d, D_(l, "hn"))
                for c in range(TT):
                    for pr in range(2):
                        ins = nc.tensor.transpose(psum_pair(psum, pr)[:, P * c:P * c + P],
                                                  ML["kt"][:, c, P * pr:P * pr + P], ident)
                ins.then_inc(ml_t, 1)
                pe.wait_ge(ml_d, D_(l, "out"))

            def ma_pe(l, full):
                for n, (off, cnt) in enumerate(((MA_CQ, 3), (MA_CKV, 2))):
                    if n:
                        pe.wait_ge(ma_d, MD_(l, "cq"))
                    for i in range(cnt):
                        u = u0(l, off) + i
                        unit(u)
                        feature_unit(u, i, ranges(True))
                    for i in range(cnt):
                        pe.wait_ge(ma_a, MA_A(l, "s%d" % (3 * n + i)))
                        for r0, r1 in ranges(True):
                            ins = mm(psum_pair(psum, 3)[:, r0:r1], ones, MA["sqq"][:, r0:r1],
                                     start=i == 0, stop=i == cnt - 1)
                        ins.then_inc(ma_t, 1)
                u = u0(l, MA_KR)
                unit(u)
                feature_unit(u, 2, ranges(True))
                wh, wl = unit(u + 1)
                pe.wait_ge(ma_d, MD_(l, "ck"))
                pe.wait_ge(ma_a, MA_A(l, "kr"))
                for t in range(TT):
                    for k in range(2):
                        ts = slice(P * t, P * t + P)
                        c = slice(512 * k, 512 * k + 512)
                        mm(bank(t), MA["ckhi"][:, k, ts], wh[:, c], start=k == 0, stop=False)
                        mm(bank(t), MA["cklo"][:, k, ts], wh[:, c], start=False, stop=False)
                        ins = mm(bank(t), MA["ckhi"][:, k, ts], wl[:, c], start=False, stop=k == 1)
                ins.then_inc(w_used, 1)

            def ma_head_pe(l, h, full):
                u = u0(l, MA_HEAD) + h // 2
                at = 512 * (h % 2)
                unit(u)
                feature_unit(u, 1, ranges(True), MA["ckhi"], MA["cklo"], m=64, nk=2, at=at + 384,
                             done=False).then_inc(ma_t, 1)
                feature_unit(u, 0, ranges(full), MA["cqhi"], MA["cqlo"], nk=3, at=at,
                             done=False).then_inc(w_used if h % 2 else ma_t, 1)
                pe.wait_ge(ma_a, MA_A(l, f"ak{h}"))
                for r0, r1 in ranges(True):
                    ins = mm(psum_pair(psum, 3)[:, r0:r1], ones[0:96, :], MA["sqk"][0:96, r0:r1], start=True, stop=True)
                ins.then_inc(ma_t, 1)
                pe.wait_ge(ma_a, MA_A(l, f"aq{h}"))
                for r0, r1 in ranges(full):
                    ins = mm(psum_pair(psum, 2)[:, r0:r1], ones[0:96, :], MA["sqq"][0:96, r0:r1], start=True, stop=True)
                ins.then_inc(ma_t, 1)

            def ff_pe(l, full):
                rr = ranges(full)
                j0 = 0
                for g, n in enumerate(FF_GROUPS):
                    b, bo = u0(l, FF_IN[g]), u0(l, FF_OUT[g])
                    gj, gx = l * HG + j0, l * XPL + (3 + g) * KT
                    pe.wait_ge(x_free, gx + 2)
                    with pe.Fori(0, n // 2) as i:
                        for jj in range(2):
                            pe.wait_ge(ff_free, i * 2 + (gj + jj + 1))
                            for ab in range(2):
                                q = 2 * jj + ab
                                pe.wait_ge(lo_done, i * 4 + (b + q + 1))
                                feature_unit(b + q, q, rr)
                    pe.wait_ge(ff_free, gj + n + 2)
                    with pe.Fori(0, KT // 2) as i:
                        for mj in range(2):
                            pe.wait_ge(lo_done, i * 2 + (bo + mj + 1))
                            pe.wait_ge(x_free, i * 2 + (gx + mj + 1))
                            feature_unit(bo + mj, mj, rr, FF["uhi"], FF["ulo"], nk=n)
                    j0 += n

            for l in range(DEPTH):
                full = l < DEPTH - 1
                mod_phase(l)
                barrier()
                norm_phase(l, 0, True)
                barrier()
                na_inputs(l)
                barrier()
                for pr in range(2):
                    na_pair(l, pr)
                    barrier()
                    for a in range(2):
                        att_pe(NA, l, "na", 2 * pr + a, NA["qhi"][:, a, :], NA["qlo"][:, a, :], NA["khi"], NA["klo"],
                               lambda k: (NA["vhi"][:, k, P * pr:P * pr + P], NA["vlo"][:, k, P * pr:P * pr + P]))
                    barrier()
                out_units(l, 0, NA_OUT, 2, NA["ohi"], NA["olo"], ranges(full))
                barrier()
                ml_pe(l, full)
                out_units(l, 1, ML_OUT, 2, ML["ohi"], ML["olo"], ranges(full))
                barrier()
                ma_pe(l, full)
                barrier()
                for h in range(MLA_HEADS):
                    ma_head_pe(l, h, full)
                    barrier()
                    att_pe(MA, l, "ma", h, MA["qhi"][0:96, 0, :], MA["qlo"][0:96, 0, :], MA["khi"][0:96, :], MA["klo"][0:96, :],
                           lambda k: (VHI[:, k, P * (h // 2):P * (h // 2) + P], VLO[:, k, P * (h // 2):P * (h // 2) + P]))
                    barrier()
                out_units(l, 2, MA_OUT, 4, hhi, hlo, ranges(full))
                barrier()
                norm_phase(l, 1, full)
                barrier()
                ff_pe(l, full)
                barrier()

        @block.vector
        def _(dve):
            V = nc.vector
            chain, nph = [0], [0]

            def seq(ins):
                chain[0] += 1
                ins.then_inc(dve_chain, 1)
                dve.wait_ge(dve_chain, chain[0])

            def barrier():
                nph[0] += 1
                dve.drain().then_inc(dve_phase, 1)
                dve.wait_ge(pe_phase, nph[0])
                dve.wait_ge(act_phase, nph[0])

            def split(hi, lo, src):
                seq(V.tensor_copy(hi, src))
                return V.tensor_tensor(lo, src, hi, ALU.subtract)

            def mod_phase(l):
                if l == 0:
                    dve.wait_ge(xin, 16 * (KT + 4))
                    V.tensor_copy(identb[:, :], ident)
                    V.tensor_copy(dirmask[:, :, :], dirm[:, :].rearrange("p (d s) -> p d s", d=2))
                    seq(V.tensor_scalar(lc[:, :, C_NAQ:C_NAQ + 2], lc[:, :, C_NAQ:C_NAQ + 2],
                                        HEAD_DIM ** -0.5, None, ALU.mult))
                dve.wait_ge(mod_tr, l + 1)
                for c in range(2):
                    seq(V.tensor_tensor(mods[:, l, :, c], bank(2)[:, c:96:2], lc[:, l, C_BMOD:C_BMOD + 48], ALU.add))
                for w in range(2):
                    for c in range(2):
                        ins = V.scalar_tensor_tensor(amix[:, l, w, :, c], mods[:, l, 24 * w + 8:24 * w + 16, c], 1.0,
                                                     lc[:, l, C_GMIX + 8 * w:C_GMIX + 8 * w + 8], ALU.add, ALU.mult)
                seq(ins)

            def norm_phase(l, which, full):
                n0 = 16 * l + 8 * which
                rr = ranges(full)
                dve.wait_ge(r_done, 2 * l + which + 1)

                def lower(k):
                    dve.wait_ge(h_hi, n0 + k + 1)
                    for r0, r1 in rr:
                        ins = V.scalar_tensor_tensor(hlo[:, k, r0:r1], NRM["t"][:, k % 2, r0:r1],
                                                     mods[:, l, 24 * which + k, cls(r0):cls(r0) + 1],
                                                     hhi[:, k, r0:r1], ALU.add, ALU.subtract)
                    ins.then_inc(h_lo, 1)
                for k in range(KT):
                    if k >= 2:
                        dve.wait_ge(h_lo, n0 + k - 1)
                    for r0, r1 in rr:
                        ins = V.scalar_tensor_tensor(NRM["t"][:, k % 2, r0:r1], xres[:, k, r0:r1],
                                                     amix[:, l, which, k, cls(r0):cls(r0) + 1],
                                                     NRM["r"][:, r0:r1], ALU.mult, ALU.mult)
                    ins.then_inc(t_done, 1)
                    if k:
                        lower(k - 1)
                lower(KT - 1)

            def out_add(l, part, ubase, nk, full, which=0):
                per = UW // (nk * P)
                for m in range(KT):
                    if m % per == per - 1:
                        dve.wait_ge(w_used, u0(l, ubase) + m // per + 1)
                    else:
                        dve.wait_ge(o_ps, OPS(l, part) + m - m // per)
                    for r0, r1 in ranges(full):
                        ins = V.scalar_tensor_tensor(xres[:, m, r0:r1], psum_pair(psum, m % 4)[:, r0:r1],
                                                     mods[:, l, 16 + m, cls(r0):cls(r0) + 1],
                                                     xres[:, m, r0:r1], ALU.mult, ALU.add)
                    ins.then_inc(x_free, 1)

            def na_inputs(l):
                for b in range(3):
                    dve.wait_ge(ev_a, 3 * l + b + 1)
                    V.tensor_tensor(NA["vlo"][:, 2 * b:2 * b + 2, :], bank(b).rearrange("p (t n) -> p t n", t=2),
                                    NA["vhi"][:, 2 * b:2 * b + 2, :], ALU.subtract)
                for g in range(16):
                    dve.wait_ge(bias_ps, 16 * l + g + 1)
                    for half in range(2):
                        rs = slice(64 * half, 64 * half + 64)
                        src = bank(4 + g % 4)[rs, 0:240].rearrange("p (i h r) -> p h r i", i=4, h=NA_HEADS)
                        m = colmask[rs, 4 * g:4 * g + 4].unsqueeze(1).broadcast_to([64, NDR, 4])
                        for h in range(NA_HEADS):
                            ins = V.tensor_tensor(NA["bias"][rs, h, half:half + NDR, 4 * g:4 * g + 4],
                                                  src[:, h, :, :], m, ALU.add)
                        ins.then_inc(bias_ev, 1)

            def na_pair(l, pr):
                for j in (0, 1):
                    n = NAJ[l, pr, j]
                    dve.wait_ge(rs2, n + 1)
                    src = psum_pair(psum, 2 + j)
                    for a in range(2 if j == 0 else 1):
                        g = C_NAK if j else C_NAQ + a
                        seq(V.scalar_tensor_tensor(NA["t"][:, :], src, lc[:, l, g:g + 1], NA["r"][:, :], ALU.mult, ALU.mult))
                        hi, lo = (NA["khi"][:, :], NA["klo"][:, :]) if j else (NA["qhi"][:, a, :], NA["qlo"][:, a, :])
                        ins = split(hi, lo, NA["t"][:, :])
                        if a == 0 and j == 0:
                            seq(ins)
                    ins.then_inc(ev_d, 1)
                dve.wait_ge(ev_d, NAJ[l, pr, 1] + 1)

            def att_dve(S, l, kind, h, scale, dst_hi, dst_lo):
                steps = PLAN[l, kind, h]

                def max_of(s, b, blk, qt, nk):
                    dve.wait_ge(s_ps, s + 1)
                    if s >= 2:
                        dve.wait_ge(s_p, s - 1)
                    sc = psum_pair(psum, s % 2)
                    st = stat[:, s % 2, :]
                    if kind == "na" and blk:
                        t = (blk - 1) * 2 + qt
                        win = S["bias"][:, h, NA_WIN_R - 1 - 2 * t:2 * NA_WIN_R - 1 - 2 * t, :].rearrange("p r c -> p (r c)")
                        V.tensor_tensor_reduce(S["s2"][:, s % 2, :], sc[:, CTX_LEN:], win, 1.0, NEG,
                                               ALU.add, ALU.max, st[:, 0:1])
                        seq(V.tensor_reduce(st[:, 1:2], sc[:, 0:CTX_LEN], AX.X, ALU.max))
                        V.tensor_scalar(st[:, 2:3], st[:, 0:1], st[:, 1:2], -1.0, ALU.max, ALU.mult).then_inc(s_nmx, 1)
                    else:
                        seq(V.tensor_reduce(st[:, 0:1], sc[:, 0:nk * P], AX.X, ALU.max))
                        V.tensor_scalar(st[:, 2:3], st[:, 0:1], -scale, None, ALU.mult).then_inc(s_nmx, 1)

                def rs_of(s, b, blk, qt, nk):
                    dve.wait_ge(s_exp, s + 1)
                    st = stat[:, s % 2, :]
                    if kind == "na" and blk:
                        seq(V.tensor_tensor(st[:, 4:5], st[:, 4:5], st[:, 5:6], ALU.add))
                    V.reciprocal(st[:, 6:7], st[:, 4:5]).then_inc(s_rs, 1)

                def lo_of(s, b, blk, qt, nk):
                    dve.wait_ge(pt_hi, s + 1)
                    V.tensor_tensor(S["ptlo"][:, 0, 0:nk, P * qt:P * qt + P],
                                    psum_pair(psum, 2)[:, 0:nk * P].rearrange("p (k q) -> p k q", q=P),
                                    S["pthi"][:, 0, 0:nk, P * qt:P * qt + P], ALU.subtract).then_inc(pt_lo, 1)

                def o_of(s, b, blk, qt, nk):
                    dve.wait_ge(pv_ps, b + 1)
                    rows = slice(64 * (h % 2), 64 * (h % 2) + 64)
                    cols_ = slice(256 * blk, 256 * blk + 256)
                    split(dst_hi[rows, cols_], dst_lo[rows, cols_], bank(6 + b % 2)[rows, 0:256]).then_inc(o_lo, 1)

                for n, st in enumerate(steps):
                    max_of(*st)
                    if n:
                        lo_of(*steps[n - 1])
                    rs_of(*st)
                    if n >= 3 and steps[n - 3][3] == 1:
                        o_of(*steps[n - 3])
                lo_of(*steps[-1])
                if len(steps) >= 4:
                    pass
                for st in steps[-3:]:
                    if st[3] == 1:
                        o_of(*st)

            def ml_dve(l, full):
                rows, tm, e, va, qk, hin = ML["rows"], ML["tm"], ML["e"], ML["va"], ML["qk"], ML["hin"]
                small = ML["small"]
                V.memset(rows[:, 3:5, :], 0.0)
                V.memset(small[:, :, :], 0.0)
                V.memset(va[:, :, :, 64:65], 1.0)
                dve.wait_ge(small_in, SMALLS["ml", l])
                dve.wait_ge(w_used, u0(l, ML_G) + 1)
                V.tensor_scalar(rows[:, 0, :], psum_pair(psum, 0)[0:36, :], lc[0:36, l, C_GM:C_GM + 1],
                                lc[0:36, l, C_GI:C_GI + 1], ALU.mult, ALU.add)
                V.tensor_scalar(rows[:, 1, :], psum_pair(psum, 0)[64:100, :], lc[0:36, l, C_GM:C_GM + 1],
                                lc[0:36, l, C_GF:C_GF + 1], ALU.mult, ALU.add).then_inc(ml_d, 1)

                def conv(i):
                    dve.wait_ge(w_used, u0(l, ML_QK) + i + 1)
                    src, y = psum_pair(psum, (i + 1) % 4), qk[:, i, :]
                    w = [lc[:, l, C_CONV + 4 * i + j:C_CONV + 4 * i + j + 1] for j in range(4)]
                    seq(V.tensor_scalar(y, src, w[1], w[3], ALU.mult, ALU.add))
                    for r0, r1 in ranges(True):
                        V.scalar_tensor_tensor(y[:, r0 + 1:r1], src[:, r0:r1 - 1], w[0], y[:, r0 + 1:r1],
                                               ALU.mult, ALU.add)
                    seq(V.drain())
                    for r0, r1 in ranges(True):
                        ins = V.scalar_tensor_tensor(y[:, r0:r1 - 1], src[:, r0 + 1:r1], w[2], y[:, r0:r1 - 1],
                                                     ALU.mult, ALU.add)
                    ins.then_inc(ml_d, 1)

                conv(0)
                dve.wait_ge(ml_a, A_(l, "sp"))
                seq(V.scalar_tensor_tensor(rows[:, 1, :], rows[:, 1, :], 0.0, rows[:, 2, :], ALU.min, ALU.subtract))
                def scan(d, out_row, in0, in1, op0, op1, r0, r1, init):
                    rs = slice(32 * d, 32 * d + 4)
                    step = -1 if d else 1
                    f = lambda x: x[rs, r0:r1][:, ::step]
                    return V.tensor_tensor_scan(f(rows[:, out_row, :]), f(in0), f(in1), init, op0, op1)
                lf, gi, b, m = (rows[:, j, :] for j in (1, 0, 3, 4))
                for d in range(2):
                    scan(d, 3, ML["mask"], lf, ALU.mult, ALU.add, 0, TOK, 0.0)
                scan(0, 4, lf, gi, ALU.add, ALU.max, 0, TOK, 0.0)
                seq(scan(1, 4, lf, gi, ALU.add, ALU.max, 0, CTX_LEN, 0.0))
                seq(scan(1, 4, lf, gi, ALU.add, ALU.max, CTX_LEN, TOK, m[32:36, 0:1]))
                seq(V.tensor_tensor(rows[:, 2, :], b, m, ALU.subtract))
                seq(V.tensor_tensor(rows[:, 0, :], gi, b, ALU.subtract))
                c_, L = rows[:, 2, :], ML_CHUNK
                V.tensor_copy(small[0:4, 0, 1:TT], m[0:4, L - 1:TOK - 1:L])
                V.tensor_copy(small[32:36, 0, 0:1], m[32:36, L:L + 1])
                V.tensor_copy(small[32:36, 0, CT:TT - 1], m[32:36, CTX_LEN + L:TOK:L])
                V.tensor_copy(small[32:36, 0, TT - 1:TT], m[32:36, 0:1])
                V.tensor_copy(small[0:4, 1, :], c_[0:4, L - 1:TOK:L])
                seq(V.tensor_copy(small[32:36, 1, :], c_[32:36, 0:TOK:L]))
                bc = lambda x: x.unsqueeze(2).broadcast_to([36, TT, L])
                ch = lambda x: x.rearrange("p (c s) -> p c s", c=TT)
                V.tensor_tensor(ch(rows[:, 5, :]), ch(c_), bc(small[:, 0, :]), ALU.add)
                V.tensor_tensor(ch(rows[:, 1, :]), ch(rows[:, 0, :]), bc(small[:, 1, :]), ALU.add)
                seq(V.tensor_scalar(rows[:, 4, :], m, -1.0, None, ALU.mult))
                V.tensor_tensor(small[:, 2, :], small[:, 0, :], small[:, 1, :], ALU.add).then_inc(ml_d, 1)
                for i in range(1, 4):
                    conv(i)
                dve.wait_ge(ml_a, A_(l, "cv3"))
                V.tensor_scalar(qk[:, 2:4, :], qk[:, 2:4, :], HEAD_DIM ** -0.5, None, ALU.mult).then_inc(ml_d, 1)
                for r in range(8):
                    h, d = r // 2, r % 2
                    dve.wait_ge(ml_a, A_(l, f"e{r}"))
                    dve.wait_ge(ml_t, T_(l, f"st{r - r % 2}"))
                    V.tensor_tensor(e[:, d, :], e[:, d, :], psum_pair(psum, 0), ALU.mult).then_inc(ml_d, 1)

                def keys(n):
                    if n >= 2:
                        dve.wait_ge(ml_t, T_(l, f"u{n - 2}"))
                    for d in range(2):
                        c = CHUNKS[d][n]
                        ins = V.tensor_tensor(ML["kw"][:, n % 2, d, :].rearrange("p (h n) -> p h n", h=4),
                                              ML["kt"][:, c, :].rearrange("p (h n) -> p h n", h=4),
                                              tm[:, c, 3, 32 * d:32 * d + 4].unsqueeze(2).broadcast_to([P, 4, 64]),
                                              ALU.mult)
                    ins.then_inc(ml_d, 1)

                def state(n):
                    dve.wait_ge(ml_t, T_(l, f"u{n}"))
                    if n >= 2:
                        dve.wait_ge(ml_t, T_(l, f"x{n - 1}"))
                    for d in range(2):
                        c = CHUNKS[d][n]
                        um = ML["um"] if n else ML["st"][:, 1, 2 * d:2 * d + 2, :]
                        ins = V.tensor_tensor(um[:, :, :] if n else um,
                                              bank(4 + 2 * (n % 2) + d)[:, 0:260].rearrange("p (a n) -> p a n", a=2),
                                              ML["blk"][:, :].unsqueeze(1).broadcast_to([P, 2, 130]), ALU.mult)
                        if n:
                            seq(ins)
                            for pr in range(2):
                                x = 2 * d + pr
                                ins = V.scalar_tensor_tensor(ML["st"][:, (n + 1) % 2, x, :], ML["st"][:, n % 2, x, :],
                                                             ML["dec"][:, x, c:c + 1], ML["um"][:, pr, :],
                                                             ALU.mult, ALU.add)
                            if d == 0:
                                seq(ins)
                    ins.then_inc(ml_d, 1)
                    dve.wait_ge(ml_d, D_(l, f"s{n}"))

                def inter(n):
                    dve.wait_ge(ml_t, T_(l, f"x{n}"))
                    for d in range(2):
                        c = CHUNKS[d][n]
                        seq(V.tensor_tensor(ML["hs"][:, d, :, :],
                                            bank(2 * (n % 2) + d)[:, 0:260].rearrange("p (h n) -> p h n", h=4),
                                            tm[:, c, 1, 32 * d:32 * d + 4].unsqueeze(2).broadcast_to([P, 4, 65]),
                                            ALU.mult))
                        ins = V.tensor_tensor(hin[:, 4 * d:4 * d + 4, c, :], hin[:, 4 * d:4 * d + 4, c, :],
                                              ML["hs"][:, d, :, :], ALU.add)
                        if d == 0:
                            seq(ins)
                    ins.then_inc(ml_d, 1)

                dve.wait_ge(ml_a, A_(l, "h7"))
                keys(0)
                for n in range(TT):
                    if n < TT - 2:
                        keys(n + 1)
                    if n < TT - 1:
                        state(n)
                    if n:
                        inter(n)
                dve.wait_ge(ml_d, D_(l, f"x{TT - 1}"))
                den = ML["den"]
                seq(V.scalar_tensor_tensor(den[:, :, :], hin[:, :, :, 64], -1.0, hin[:, :, :, 64], ALU.mult, ALU.max))
                for d in range(2):
                    ins = V.tensor_tensor(den[:, 4 * d:4 * d + 4, :], den[:, 4 * d:4 * d + 4, :],
                                          tm[:, :, 2, 32 * d:32 * d + 4].rearrange("p c h -> p h c"), ALU.max)
                seq(ins)
                seq(V.reciprocal(den[:, :, :], den[:, :, :]))
                seq(V.tensor_tensor(hin[:, :, :, 0:64], hin[:, :, :, 0:64],
                                    den[:, :, :].unsqueeze(3).broadcast_to([P, 8, TT, 64]), ALU.mult))
                V.tensor_tensor(hin[:, 0:4, :, 0:64], hin[:, 0:4, :, 0:64], hin[:, 4:8, :, 0:64], ALU.add)\
                    .then_inc(ml_d, 1)
                dve.wait_ge(ml_a, A_(l, "sq"))
                sq = e[:, :, :].rearrange("p a t -> p (a t)").rearrange("p (h c n) -> p h c n", h=4, c=TT)
                V.tensor_reduce(ML["ssq"][:, :, :], sq, AX.X, ALU.add).then_inc(ml_d, 1)
                dve.wait_ge(ml_a, A_(l, "rstd"))
                V.tensor_tensor(ML["kt"][:, :, :].rearrange("p c (h n) -> p h c n", h=4), hin[:, 0:4, :, 0:64],
                                ML["ssq"][:, :, :].unsqueeze(3).broadcast_to([P, 4, TT, 64]), ALU.mult).then_inc(ml_d, 1)
                dve.wait_ge(ml_t, T_(l, "ht"))
                for pr in range(2):
                    seq(V.scalar_tensor_tensor(e[:, pr, :], psum_pair(psum, pr), lc[:, l, C_HG + pr:C_HG + pr + 1],
                                               ML["osig"][:, pr, :], ALU.mult, ALU.mult))
                    ins = split(ML["ohi"][:, pr, :], ML["olo"][:, pr, :], e[:, pr, :])
                ins.then_inc(ml_d, 1)

            def ma_dve(l, full):
                for n, (cnt, col, hi, lo) in enumerate(((3, C_CQ, MA["cqhi"], MA["cqlo"]), (2, C_CKV, MA["ckhi"], MA["cklo"]))):
                    dve.wait_ge(ma_a, MA_A(l, f"r{n}"))
                    for i in range(cnt):
                        seq(V.scalar_tensor_tensor(MA["t"][:, :], psum_pair(psum, i), lc[:, l, col + i:col + i + 1],
                                                   MA["r"][:, n, :], ALU.mult, ALU.mult))
                        ins = split(hi[:, i, :], lo[:, i, :], MA["t"][:, :])
                        if i < cnt - 1:
                            seq(ins)
                    ins.then_inc(ma_d, 1)
                    dve.wait_ge(ma_d, MD_(l, ("cq", "ck")[n]))
                dve.wait_ge(small_in, SMALLS["ma", l])
                for t in range(TT):
                    dve.wait_ge(ma_a, MA_A(l, f"v{t}"))
                    V.tensor_tensor(VLO[:, t, :], bank(t), VHI[:, t, :], ALU.subtract)

            def ma_head_dve(l, h, full):
                q0 = 0 if full else CTX_LEN
                X = slice(CTX_LEN, TOK)
                for what, buf, q, ri in (("rk", MA["t"], 0, 1), ("rq", MA["t2"], q0, 0)):
                    dve.wait_ge(ma_a, MA_A(l, f"{what}{h}"))
                    g = C_MK if ri else C_MQ
                    if ri:
                        V.scalar_tensor_tensor(buf[0:64, :], psum_pair(psum, 1)[0:64, :], lc[0:64, l, g:g + 1],
                                               MA["r"][0:64, 1, :], ALU.mult, ALU.mult)
                        ins = V.scalar_tensor_tensor(buf[64:128, :], MA["kr"][64:128, :], lc[64:128, l, g:g + 1],
                                                     MA["r"][64:128, 1, :], ALU.mult, ALU.mult)
                    else:
                        ins = V.scalar_tensor_tensor(buf[:, q:], psum_pair(psum, 0)[:, q:], lc[:, l, g:g + 1],
                                                     MA["r"][:, 0, q:], ALU.mult, ALU.mult)
                    seq(ins)
                    V.tensor_tensor(MA["p"][64:96, 0, 0:SEQ], buf[96:128, X], MA["rope"][96:128, 1, :], ALU.mult)
                    seq(V.tensor_tensor(MA["p"][64:96, 1, 0:SEQ], buf[64:96, X], MA["rope"][64:96, 0, :], ALU.mult))
                    seq(V.tensor_tensor(buf[64:96, X], MA["p"][64:96, 0, 0:SEQ], MA["p"][64:96, 1, 0:SEQ], ALU.add))
                    hi, lo = (MA["khi"], MA["klo"]) if ri else (MA["qhi"][:, 0, :], MA["qlo"][:, 0, :])
                    split(hi[0:96, q:], lo[0:96, q:], buf[0:96, q:]).then_inc(ma_d, 1)
                    dve.wait_ge(ma_d, MD_(l, ("dq", "dk")[ri] + str(h)))

            def ff_dve(l, full):
                q0 = 0 if full else CTX_LEN
                j0 = 0
                for g, n in enumerate(FF_GROUPS):
                    b, bo = u0(l, FF_IN[g]), u0(l, FF_OUT[g])
                    gj, gx = l * HG + j0, l * XPL + (3 + g) * KT
                    with dve.Fori(0, n // 2) as i:
                        for jj in range(2):
                            dve.wait_ge(ff_sa, i * 2 + (gj + jj + 1))
                            V.tensor_tensor(FF["uf"][:, jj, q0:], FF["sa"][:, jj, q0:],
                                            psum_pair(psum, 2 * jj + 1)[:, q0:], ALU.mult).then_inc(ff_uf, 1)
                            dve.wait_ge(ff_uf, i * 2 + (gj + jj + 1))
                            V.tensor_copy(FF["uhi"][:, bass.ds(i * 2 + jj, 1), q0:].rearrange("p o t -> p (o t)"),
                                          FF["uf"][:, jj, q0:]).then_inc(ff_uhi, 1)
                            dve.wait_ge(ff_uhi, i * 2 + (gj + jj + 1))
                            V.tensor_tensor(FF["ulo"][:, bass.ds(i * 2 + jj, 1), q0:].rearrange("p o t -> p (o t)"),
                                            FF["uf"][:, jj, q0:],
                                            FF["uhi"][:, bass.ds(i * 2 + jj, 1), q0:].rearrange("p o t -> p (o t)"),
                                            ALU.subtract).then_inc(ff_free, 1)
                    with dve.Fori(0, KT // 2) as i:
                        for mj in range(2):
                            dve.wait_ge(w_used, i * 2 + (bo + mj + 1))
                            for r0, r1 in ranges(full):
                                xm = xres[:, bass.ds(i * 2 + mj, 1), r0:r1].rearrange("p o t -> p (o t)")
                                gate = mods[:, l, bass.ds(i * 2 + (40 + mj), 1), cls(r0):cls(r0) + 1]\
                                    .rearrange("p o t -> p (o t)")
                                ins = V.scalar_tensor_tensor(xm, psum_pair(psum, mj)[:, r0:r1], gate, xm,
                                                             ALU.mult, ALU.add)
                            ins.then_inc(x_free, 1)
                    j0 += n

            V.memset(eps[:, :], EPS).then_inc(ff_free, 2)
            V.memset(stat[:, :, :], 0.0).then_inc(x_free, 2)
            for l in range(DEPTH):
                full = l < DEPTH - 1
                mod_phase(l)
                barrier()
                norm_phase(l, 0, True)
                barrier()
                na_inputs(l)
                barrier()
                for pr in range(2):
                    na_pair(l, pr)
                    barrier()
                    for a in range(2):
                        att_dve(NA, l, "na", 2 * pr + a, 1.0, NA["ohi"][:, pr, :], NA["olo"][:, pr, :])
                    barrier()
                out_add(l, 0, NA_OUT, 2, full)
                barrier()
                ml_dve(l, full)
                out_add(l, 1, ML_OUT, 2, full)
                barrier()
                ma_dve(l, full)
                barrier()
                for h in range(MLA_HEADS):
                    ma_head_dve(l, h, full)
                    barrier()
                    att_dve(MA, l, "ma", h, QK_DIM ** -0.5, hhi[:, h // 2, :], hlo[:, h // 2, :])
                    barrier()
                out_add(l, 2, MA_OUT, 4, full)
                barrier()
                norm_phase(l, 1, full)
                barrier()
                ff_dve(l, full)
                barrier()


def weight_units(w_in, w_uq, w_ukv, w_out, w_ffn_in, w_ffn_out):
    na, ml = NA_HEADS * HEAD_DIM, ML_HEADS * HEAD_DIM
    o_v, o_ml = 2 * na, 3 * na
    o_g = o_ml + 4 * ml
    o_cq = o_g + NG
    o_ckv, o_kr = o_cq + Q_LORA, o_cq + Q_LORA + KV_LORA
    s = np.zeros((DEPTH, UNITS, P, UW), np.float32)

    def rows(w):
        return w.reshape(-1, P, w.shape[1]).transpose(1, 0, 2)

    for l in range(DEPTH):
        def put(u, *parts):
            flat = np.concatenate([x.reshape(P, -1) for x in parts], axis=1)
            s[l, u, :, :flat.shape[1]] = flat
        wi = rows(w_in[l])
        tile = lambda c: wi[:, :, c:c + P]
        for half in range(2):
            put(NA_V + half, wi[:, 4 * half:4 * half + 4, o_v:o_v + na])
            put(ML_V + half, wi[:, 4 * half:4 * half + 4, o_ml + 2 * ml:o_ml + 3 * ml])
        for pr in range(2):
            put(NA_QK + 2 * pr, tile(P * pr))
            put(NA_QK + 2 * pr + 1, tile(na + P * pr))
            put(ML_QK + pr, tile(o_ml + P * pr))
            put(ML_QK + 2 + pr, tile(o_ml + ml + P * pr))
            put(ML_O + pr, tile(o_ml + 3 * ml + P * pr))
        g = np.zeros((P, KT, P), np.float32)
        for at, n in ((0, 0), (64, 1), (32, 2), (96, 3)):
            g[:, :, at:at + ML_HEADS] = wi[:, :, o_g + ML_HEADS * n:o_g + ML_HEADS * (n + 1)]
        put(ML_G, g)
        for i in range(3):
            put(MA_CQ + i, tile(o_cq + P * i))
        for i in range(2):
            put(MA_CKV + i, tile(o_ckv + P * i))
        r = np.zeros((P, KT, P), np.float32)
        h2 = ROPE // 2
        r[:, :, NOPE:QK_DIM] = wi[:, :, o_kr:o_kr + ROPE]
        r[:, :, QK_DIM:QK_DIM + h2] = wi[:, :, o_kr + h2:o_kr + ROPE]
        r[:, :, QK_DIM + h2:] = wi[:, :, o_kr:o_kr + h2]
        put(MA_KR, r)
        uq = rows(w_uq[l]).reshape(P, Q_LORA // P, MLA_HEADS, QK_DIM)
        uq = np.concatenate([uq, uq[..., NOPE + h2:], uq[..., NOPE:NOPE + h2]], axis=-1)
        ukv = rows(w_ukv[l]).reshape(P, KV_LORA // P, MLA_HEADS, NOPE + V_DIM)
        put(MA_V, ukv[..., NOPE:])
        for j in range(MLA_HEADS // 2):
            put(MA_HEAD + j, uq[:, :, 2 * j], ukv[:, :, 2 * j, :NOPE], uq[:, :, 2 * j + 1], ukv[:, :, 2 * j + 1, :NOPE])
        wo = rows(w_out[l]).reshape(P, KT, KT, P)
        for j in range(2):
            put(NA_OUT + j, wo[:, 0:2, 4 * j:4 * j + 4].transpose(0, 2, 1, 3))
            put(ML_OUT + j, wo[:, 2:4, 4 * j:4 * j + 4].transpose(0, 2, 1, 3))
        for j in range(4):
            put(MA_OUT + j, wo[:, 4:8, 2 * j:2 * j + 2].transpose(0, 2, 1, 3))
        fi, fo = rows(w_ffn_in[l]), rows(w_ffn_out[l])
        j0 = 0
        for g_, n in enumerate(FF_GROUPS):
            for j in range(n):
                put(FF_IN[g_] + 2 * j, fi[:, :, P * (j0 + j):P * (j0 + j) + P])
                put(FF_IN[g_] + 2 * j + 1, fi[:, :, D_FF + P * (j0 + j):D_FF + P * (j0 + j) + P])
            for m in range(KT):
                put(FF_OUT[g_] + m, fo[:, j0:j0 + n, P * m:P * m + P])
            j0 += n
    return s.reshape(DEPTH * UNITS, P, UW)


def columns(g_mix, g_ffn, b_mod, na_qk_gain, b_gate, ml_conv_w, ml_conv_b, ml_head_gain, mla_gq, mla_gkv, mla_qk_gain):
    c = np.zeros((P, DEPTH, NCOL), np.float32)
    tiles = lambda v: v.reshape(-1, P).T
    for l in range(DEPTH):
        c[:, l, C_GMIX:C_GMIX + KT] = tiles(g_mix[l])
        c[:, l, C_GFFN:C_GFFN + KT] = tiles(g_ffn[l])
        c[:, l, C_BMOD:C_BMOD + 48] = tiles(b_mod[l])
        c[0:64, l, C_NAQ] = na_qk_gain[l, 0]
        c[64:128, l, C_NAQ + 1] = na_qk_gain[l, 0]
        c[0:64, l, C_NAK] = c[64:128, l, C_NAK] = na_qk_gain[l, 1]
        g = b_gate[l].reshape(4, ML_HEADS)
        for d in range(2):
            c[32 * d:32 * d + ML_HEADS, l, C_GI] = g[2 * d]
            c[32 * d:32 * d + ML_HEADS, l, C_GF] = g[2 * d + 1]
            c[32 * d:32 * d + ML_HEADS, l, C_GM] = 1.0
        for i in range(4):
            for j in range(3):
                c[:, l, C_CONV + 4 * i + j] = ml_conv_w[l, j, P * i:P * i + P]
            c[:, l, C_CONV + 4 * i + 3] = ml_conv_b[l, P * i:P * i + P]
        c[:, l, C_HG:C_HG + 2] = tiles(ml_head_gain[l].reshape(-1))
        c[:, l, C_CQ:C_CQ + 3] = tiles(mla_gq[l])
        c[:, l, C_CKV:C_CKV + 2] = tiles(mla_gkv[l])
        for n, col in ((0, C_MQ), (1, C_MK)):
            g = mla_qk_gain[l, n]
            h2 = ROPE // 2
            c[:, l, col] = np.concatenate([g, g[NOPE + h2:], g[NOPE:NOPE + h2]])
    return c


def tables():
    f = np.zeros((P, 3 * P + 256 + 64), np.float32)
    f[:, 0:P] = np.eye(P)
    f[:, P:2 * P] = 1.0
    for a in range(2):
        f[64 * a:64 * a + 64, 2 * P + 64 * a:2 * P + 64 * a + 64] = 1.0
    for i in range(4):
        for j in range(NDC):
            f[32 * i + j, 3 * P + 75 + i - j] = 1.0
    col = np.arange(GRID_W)
    start = np.clip(col - NA_WIN_C // 2, 0, GRID_W - NA_WIN_C)
    inside = (col[None, :] >= start[:, None]) & (col[None, :] < start[:, None] + NA_WIN_C)
    f[:, 3 * P + 256:] = np.tile(np.where(inside, 0.0, NEG), (2, 1))
    rope = np.zeros((P, 2 * SEQ + 130), np.float32)
    nf = ROPE // 4
    inv = (np.float32(ROPE_BASE) ** (-np.arange(nf, dtype=np.float32) / np.float32(nf))).astype(np.float32)
    t = np.arange(SEQ)
    ang = np.concatenate([(t // GRID_W).astype(np.float32)[:, None] * inv, (t % GRID_W).astype(np.float32)[:, None] * inv], -1)
    cos, sin = np.cos(ang).T, np.sin(ang).T
    rope[64:80, 0:SEQ] = rope[80:96, 0:SEQ] = cos
    rope[96:112, SEQ:2 * SEQ] = -sin
    rope[112:128, SEQ:2 * SEQ] = sin
    rope[0:64, 2 * SEQ:2 * SEQ + 65] = 1.0
    rope[64:128, 2 * SEQ + 65:] = 1.0
    gate = np.zeros((36, 12 * P + TOK), np.float32)
    for d in range(2):
        for h in range(ML_HEADS):
            gate[32 * d + h, P * (4 * d + h):P * (4 * d + h) + P] = 1.0
            x = 8 + 2 * d + h // 2
            gate[32 * d + h, P * x + 64 * (h % 2):P * x + 64 * (h % 2) + 64] = 1.0
    tok = np.arange(TOK)
    gate[0:4, 12 * P:] = tok % ML_CHUNK != 0
    gate[32:36, 12 * P:] = tok % ML_CHUNK != ML_CHUNK - 1
    direction = np.zeros((P, 2 * P), np.float32)
    s, q = np.meshgrid(np.arange(P), np.arange(P), indexing="ij")
    direction[:, 0:P] = np.where(s <= q, 0.0, NEG)
    direction[:, P:] = np.where(s >= q, 0.0, NEG)
    return f, rope, gate, direction


def arrays_of(x, c, ctx, c_ctx, w_mod, b_mod, g_mix, g_ffn, w_in, b_gate, na_qk_gain, na_rpb, ml_conv_w, ml_conv_b,
              ml_head_gain, mla_gq, mla_gkv, w_uq, w_ukv, mla_qk_gain, w_out, w_ffn_in, w_ffn_out):
    n = np.asarray
    fm = lambda a: n(a).T.reshape(KT, P, -1).transpose(1, 0, 2)
    f, rope, gate, direction = tables()
    rpb = np.zeros((DEPTH, 4, 32, 4, NA_HEADS * NDR), np.float32)
    for i in range(4):
        rpb[:, i, 0:NDC, i] = n(na_rpb).reshape(DEPTH, NA_HEADS * NDR, NDC).transpose(0, 2, 1)
    return {
        "x_t": np.concatenate([fm(n(ctx)[0]), fm(n(x)[0])], axis=2),
        "c_t": fm(np.stack([n(c)[0], n(c_ctx)])),
        "w_mod": n(w_mod).reshape(DEPTH, KT, P, MODU, 512).transpose(0, 3, 2, 1, 4),
        "w_stream": weight_units(n(w_in), n(w_uq), n(w_ukv), n(w_out), n(w_ffn_in), n(w_ffn_out)),
        "cols": columns(*(n(a) for a in (g_mix, g_ffn, b_mod, na_qk_gain, b_gate, ml_conv_w, ml_conv_b, ml_head_gain,
                                         mla_gq, mla_gkv, mla_qk_gain))),
        "rpb": rpb.reshape(DEPTH, P, 4 * NA_HEADS * NDR),
        "c_f32": f, "c_rope": rope, "c_gate": gate, "c_dir": direction,
    }


def kernel(**inputs):
    import concourse.bacc as bacc
    from concourse.bass_utils import run_bass_kernel_spmd

    nc = bacc.Bacc("TRN2", target_bir_lowering=False, num_devices=1)
    arrays = {k: np.ascontiguousarray(v) for k, v in arrays_of(**inputs).items()}
    aps = [nc.dram_tensor(k, v.shape, mybir.dt.from_np(v.dtype), kind="ExternalInput").ap() for k, v in arrays.items()]
    aps.append(nc.dram_tensor("out", (P, KT, SEQ), mybir.dt.float32, kind="ExternalOutput").ap())
    build(nc, *aps)
    r = run_bass_kernel_spmd(nc, [arrays], core_ids=[0])
    y = r.results[0]["out"]
    return np.ascontiguousarray(y.transpose(2, 1, 0).reshape(1, SEQ, D_MODEL))
```

```python
import concourse.bass as bass
from concourse import mybir
from contextlib import ExitStack
import numpy as np

D_MODEL, SEQ, CTX_LEN, DEPTH = 1024, 512, 256, 2
TOK = CTX_LEN + SEQ
GRID_W, HEAD_DIM = 64, 64
NA_HEADS, NA_WIN_R, NA_WIN_C = 4, 8, 16
ML_HEADS, ML_CHUNK = 4, 128
MLA_HEADS, NOPE, ROPE, V_DIM = 8, 64, 32, 64
QK_DIM = NOPE + ROPE
Q_LORA, KV_LORA = 384, 256
D_FF = -(-8 * D_MODEL // (3 * 256)) * 256
GRID_R = SEQ // GRID_W
EPS, ROPE_BASE = 1e-6, 10000.0
P = 128
KT = D_MODEL // P
TT = TOK // P
CT = CTX_LEN // P
NG = 4 * ML_HEADS
NDR = 2 * NA_WIN_R - 1
NDC = 2 * NA_WIN_C - 1
NEG = -1.0e30

UW = 1024
NA_V, NA_QK, NA_OUT = 0, 2, 6
ML_G, ML_QK, ML_O, ML_V, ML_OUT = 8, 9, 13, 15, 17
MA_CQ, MA_KR, MA_CKV, MA_V, MA_HEAD, MA_OUT = 19, 22, 23, 25, 26, 30
FF0 = 34
FF_GROUPS = (8, 8, 6)
assert sum(FF_GROUPS) * P == D_FF
FF_IN, FF_OUT = [], []
_u = FF0
for _n in FF_GROUPS:
    FF_IN.append(_u)
    FF_OUT.append(_u + 2 * _n)
    _u += 2 * _n + KT
UNITS = _u
RAW = 4
MODU = 12

C_GMIX, C_GFFN, C_BMOD = 0, 8, 16
C_NAQ, C_NAK = 64, 66
C_GI, C_GF, C_GM = 67, 68, 69
C_CONV = 70
C_HG = 86
C_CQ, C_CKV = 88, 91
C_MQ, C_MK = 93, 94
NCOL = 95


def psum_pair(ps, n):
    return ps[:, 1024 * n + 256:1024 * n + 1024]


def v_banks(ps, b):
    return ps[:, 1024 * b:1024 * b + 1024].rearrange("p (t n) -> p t n", t=2)[:, :, 0:256]


def build(nc, x_t, c_t, w_mod, w_stream, cols, rpb, c_f32, c_rope, c_gate, c_dir, out):
    fp32, fp32r, bf16 = mybir.dt.float32, mybir.dt.float32r, mybir.dt.bfloat16
    ALU, ACT, AX = mybir.AluOpType, mybir.ActivationFunctionType, mybir.AxisListType
    es = ExitStack()
    with es:
        def sb(name, shape, dt=fp32, stack=es):
            return stack.enter_context(nc.sbuf_tensor(name, shape, dt))

        def sem(name):
            return es.enter_context(nc.semaphore(name))

        xres = sb("xres", [P, KT, TOK])
        hhi = sb("hhi", [P, KT, TOK], fp32r)
        hlo = sb("hlo", [P, KT, TOK], fp32r)
        raw = sb("raw", [P, RAW, UW])
        whi = sb("whi", [P, 2, UW], fp32r)
        wlo = sb("wlo", [P, 2, UW], fp32r)
        consts = sb("consts", [P, 3 * P + 256 + 64])
        dirm = sb("dirm", [P, 2 * P])
        ident = consts[:, 0:P]
        ones = consts[:, P:2 * P]
        ones2 = consts[:, 2 * P:3 * P]
        band = consts[:, 3 * P:3 * P + 256]
        colmask = consts[:, 3 * P + 256:3 * P + 320]
        identb = sb("identb", [P, P], bf16)
        dirmask = sb("dirmask", [P, 2, P], bf16)
        lc = sb("lc", [P, DEPTH, NCOL])
        mods = sb("mods", [P, DEPTH, 48, 2])
        amix = sb("amix", [P, DEPTH, 2, KT, 2])
        csil = sb("csil", [P, KT, 2])
        eps = sb("eps", [P, 1])
        stat = sb("stat", [P, 2, 8])
        psum = es.enter_context(nc.psum_tensor("psum", [P, 8 * 512], fp32))

        def bank(n):
            return psum[:, 512 * n:512 * n + 512]

        def scope(fn):
            with ExitStack() as s:
                return fn(lambda name, shape, dt=fp32: sb(name, shape, dt, s))

        def mod_scope(a):
            return dict(wm=a("wm", [P, 3, KT * 512]), row=a("modrow", [2, 48 * P]))

        def norm_scope(a):
            return dict(sq=a("n_sq", [P, 2, TOK]), r=a("n_r", [P, TOK]), t=a("n_t", [P, 2, TOK]))

        def na_scope(a):
            d = dict(qhi=a("naqhi", [P, 2, TOK], fp32r), qlo=a("naqlo", [P, 2, TOK], fp32r),
                     khi=a("nakhi", [P, TOK], fp32r), klo=a("naklo", [P, TOK], fp32r),
                     vhi=a("navhi", [P, TT, 256], fp32r), vlo=a("navlo", [P, TT, 256], fp32r),
                     bias=a("nabias", [P, NA_HEADS, 16, GRID_W]),
                     ohi=a("naohi", [P, 2, TOK], fp32r), olo=a("naolo", [P, 2, TOK], fp32r),
                     rb=a("narpb", [P, 4 * NA_HEADS * NDR]))
            d.update(p=a("nap", [P, 2, TOK]), s2=a("nas2", [P, 2, 512]), dg=a("nadg", [P, 2, P]), of=a("naof", [P, 256]))
            with ExitStack() as s:
                d.update(sq=sb("nasq", [P, TOK], fp32, s), r=sb("nar", [P, TOK], fp32, s), t=sb("nat", [P, TOK], fp32, s))
            d.update(pthi=a("napthi", [P, 2, TT, 256], fp32r), ptlo=a("naptlo", [P, 2, TT, 256], fp32r))
            return d

        def ml_scope(a):
            d = dict(qk=a("mlqk", [P, 4, TOK]), osig=a("mlosig", [P, 2, TOK]),
                        va=a("mlva", [P, TT, ML_HEADS, 65]), kt=a("mlkt", [P, TT, 256]),
                        tm=a("mltm", [P, TT, 4, 36]),
                        e=a("mle", [P, 2, TOK]), hin=a("mlhin", [P, 8, TT, 65]),
                        kw=a("mlkw", [P, 2, 2, 256]), st=a("mlst", [P, 2, 4, 130]),
                        small=a("mlsmall", [36, 6, 6]), dec=a("mldec", [P, 4, 6]),
                        hs=a("mlhs", [P, 2, 4, 65]), um=a("mlum", [P, 2, 130]), sel=a("mlsel", [36, 8 * P + 4 * P]),
                        blk=a("mlblk", [P, 130]),
                        den=a("mlden", [P, 8, TT]), mask=a("mlmask", [36, TOK]), ssq=a("mlssq", [P, ML_HEADS, TT]))
            with ExitStack() as s:
                d["rows"] = sb("mlrows", [36, 6, TOK], fp32, s)
            d.update(ohi=a("mlohi", [P, 2, TOK], fp32r), olo=a("mlolo", [P, 2, TOK], fp32r))
            return d

        def ma_scope(a):
            d = dict(cqhi=a("cqhi", [P, 3, TOK], fp32r), cqlo=a("cqlo", [P, 3, TOK], fp32r),
                     ckhi=a("ckhi", [P, 2, TOK], fp32r), cklo=a("cklo", [P, 2, TOK], fp32r),
                     kr=a("krraw", [P, TOK]), sqk=a("masqk", [P, TOK]),
                     qhi=a("maqhi", [P, 2, TOK], fp32r), qlo=a("maqlo", [P, 2, TOK], fp32r),
                     khi=a("makhi", [P, 2, TOK], fp32r), klo=a("maklo", [P, 2, TOK], fp32r),
                     rope=a("marope", [P, 2, SEQ]), p=a("map", [P, 2, TOK]),
                     dg=a("madg", [P, 2, P]), of=a("maof", [P, 256]))
            with ExitStack() as s:
                d.update(sqq=sb("masqq", [P, TOK], fp32, s), t=sb("mat", [P, TOK], fp32, s),
                         t2=sb("mat2", [P, TOK], fp32, s), r=sb("mar", [P, 2, TOK], fp32, s))
            d.update(pthi=a("mapthi", [P, 2, TT, 256], fp32r), ptlo=a("maptlo", [P, 2, TT, 256], fp32r))
            return d

        def ff_scope(a):
            return dict(uhi=a("uhi", [P, 8, TOK], fp32r), ulo=a("ulo", [P, 8, TOK], fp32r),
                        sa=a("ffsa", [P, 2, TOK]), uf=a("ffuf", [P, 2, TOK]))

        MODS, NRM, NA, ML, MA, FF = (scope(f) for f in (mod_scope, norm_scope, na_scope, ml_scope, ma_scope, ff_scope))

        xin = sem("xin")
        mod_in = [sem(f"mod_in{i}") for i in range(3)]
        small_in = sem("small_in")
        raw_full = [sem(f"raw_full{i}") for i in range(RAW)]
        hi_done, lo_done = sem("hi_done"), sem("lo_done")
        w_used = sem("w_used")
        pe_phase, act_phase, dve_phase = sem("pe_phase"), sem("act_phase"), sem("dve_phase")
        act_chain, dve_chain = sem("act_chain"), sem("dve_chain")
        mod_ps, mod_row, mod_tr = sem("mod_ps"), sem("mod_row"), sem("mod_tr")
        sq_done, sq_used, st_done = sem("sq_done"), sem("sq_used"), sem("st_done")
        r_done, t_done, h_hi, h_lo = sem("r_done"), sem("t_done"), sem("h_hi"), sem("h_lo")
        s_ps, s_nmx, s_exp, s_rs = (sem(x) for x in ("scores", "negmax", "exps", "inv_rowsum"))
        t_ps, pt_hi, pt_lo = sem("probsT"), sem("probsT_hi"), sem("probsT_lo")
        inv_ps, pv_ps, o_lo = sem("inv_rows"), sem("pv"), sem("o_lo")
        x_free = sem("x_free")
        ff_free = sem("ff_free")
        ff_sa, ff_uf, ff_uhi = sem("ff_silu"), sem("ff_prod"), sem("ff_uhi")
        ev_ps, ev_a, ev_d = sem("ev_ps"), sem("ev_a"), sem("ev_d")
        out_done = sem("out_done")
        sq2, rs2 = sem("head_squares"), sem("head_rsqrt")
        bias_ps, bias_ev, o_ps = sem("bias_ps"), sem("bias_ev"), sem("o_ps")
        ml_t, ml_a, ml_d = sem("ml_tensor"), sem("ml_scalar"), sem("ml_vector")
        ma_t, ma_a, ma_d = sem("ma_tensor"), sem("ma_scalar"), sem("ma_vector")

        HG = D_FF // P
        XPL = 8 * (3 + len(FF_GROUPS))

        def u0(l, off):
            return l * UNITS + off

        def ranges(full):
            return [(CTX_LEN, TOK), (0, CTX_LEN)] if full else [(CTX_LEN, TOK)]

        def cls(r0):
            return 1 if r0 == 0 else 0

        def att_blocks(l):
            return ([0] if l < DEPTH - 1 else []) + [1, 2]

        def att_plan():
            plan, s, b = {}, 0, 0
            for l in range(DEPTH):
                for kind, heads in (("na", NA_HEADS), ("ma", MLA_HEADS)):
                    for h in range(heads):
                        steps = []
                        for blk in att_blocks(l):
                            for qt in (0, 1):
                                steps.append((s, b, blk, qt, CT if blk == 0 else TT))
                                s += 1
                            b += 1
                        plan[l, kind, h] = steps
            return plan

        PLAN = att_plan()
        NAJ = {(l, pr, j): 4 * l + 2 * pr + j for l in range(DEPTH) for pr in range(2) for j in range(2)}
        SMALLS = {(k, l): 16 * (5 * l + n) for l in range(DEPTH) for k, n in (("na", 1), ("ml", 4), ("ma", 5))}
        CHUNKS = (list(range(TT)), list(range(CT))[::-1] + list(range(CT, TT))[::-1])
        VHI = hhi[:, 4:8, :].rearrange("p k t -> p (k t)").rearrange("p (t n) -> p t n", t=TT)
        VLO = hlo[:, 4:8, :].rearrange("p k t -> p (k t)").rearrange("p (t n) -> p t n", t=TT)

        def OPS(l, part):
            return 16 * l + (0, 6, 12)[part] + 1

        def counts(names):
            at = {n: i + 1 for i, n in enumerate(names)}
            return lambda l, n: l * len(names) + at[n]

        T_ = counts(["tm", "dec", "kt0", "kt1", "kt2"]
                    + ["st0", "cr0"] + [f"{x}{r + (x != 'in')}" for r in range(8) for x in ("cr", "st", "in")
                                        if (x == "in" or r < 7) and (x != "st" or r % 2)]
                    + [f"{x}{n}" for n in range(TT) for x in ("x", "u") if (n or x == "u") and (n < TT - 1 or x == "x")]
                    + ["ht"])
        A_ = counts(["sp"] + [f"cv{i}" for i in range(4)]
                    + ["o0", "o1", "v0", "v1", "v2", "ed", "tm", "dec", "kt0", "kt1", "kt2"]
                    + ["e0"] + [f"{x}{r + (x == 'e')}" for r in range(8) for x in ("e", "h") if x == "h" or r < 7] + ["sq", "rstd"])
        D_ = counts(["gates", "cv0", "rows", "cv1", "cv2", "cv3", "k8"] + [f"p{r}" for r in range(8)] + ["kw0"]
                    + [f"{x}{n + (x == 'kw')}" for n in range(TT) for x in ("kw", "s", "x")
                       if (x == "kw" and n < TT - 2) or (x == "s" and n < TT - 1) or (x == "x" and n)]
                    + ["hsum", "ssq", "hn", "out"])
        MT_ = counts([f"c{i}" for i in range(5)]
                     + [f"{x}{h}" for h in range(MLA_HEADS) for x in ("hk", "hq", "tk", "tq") if x != "hq" or h % 2 == 0])
        MA_A = counts(["s0", "s1", "s2", "r0", "kr", "s3", "s4", "r1"] + [f"v{t}" for t in range(TT)]
                      + [f"{x}{h}" for h in range(MLA_HEADS) for x in ("ak", "aq", "rk", "rq")])
        MD_ = counts(["cq", "ck"] + [f"{x}{h}" for h in range(MLA_HEADS) for x in ("dk", "dq")])

        block = es.enter_context(nc.Block())

        @block.sync
        def _(sp):
            for k in range(KT):
                sp.dma_start(xres[:, k, :], x_t[:, k, :]).then_inc(xin, 16)
            sp.dma_start(csil[:, :, :], c_t).then_inc(xin, 16)
            sp.dma_start(consts[:, :], c_f32).then_inc(xin, 16)
            sp.dma_start(dirm[:, :], c_dir).then_inc(xin, 16)
            sp.dma_start(lc[:, :, :], cols).then_inc(xin, 16)
            def load(u, slot):
                sp.dma_start(raw[:, slot, :], w_stream[bass.ds(u, 1), :, :].rearrange("o p w -> (o p) w"))\
                    .then_inc(raw_full[slot], 16)
            for s in range(RAW):
                load(s, s)
            with sp.Fori(1, DEPTH * UNITS // RAW) as i:
                for s in range(RAW):
                    sp.wait_ge(lo_done, i * RAW + (s + 1 - RAW))
                    load(i * RAW + s, s)
            sp.wait_ge(x_free, 2 + DEPTH * XPL)
            for k in range(KT):
                sp.dma_start(out[:, k, :], xres[:, k, CTX_LEN:TOK]).then_inc(out_done, 16)
            sp.wait_ge(out_done, 16 * KT)

        @block.gpsimd
        def _(pool):
            def lo(u, q, first=False):
                pool.wait_ge(hi_done, u + 1)
                if not first:
                    pool.wait_ge(w_used, u - 1)
                nc.gpsimd.tensor_tensor(wlo[:, q % 2, :], raw[:, q % RAW, :], whi[:, q % 2, :],
                                        ALU.subtract).then_inc(lo_done, 1)
            for q in range(RAW):
                lo(q, q, first=q < 2)
            with pool.Fori(1, DEPTH * UNITS // RAW) as i:
                for q in range(RAW):
                    lo(i * RAW + q, q)

        @block.scalar
        def _(act):
            A = nc.scalar.activation
            chain, hi_next, nph, smalls = [0], [0], [0], [0]

            def seq(ins):
                chain[0] += 1
                ins.then_inc(act_chain, 1)
                act.wait_ge(act_chain, chain[0])

            def hi(u, q, first=False):
                if isinstance(u, int):
                    act.wait_ge(raw_full[q % RAW], 16 * (u // RAW + 1))
                if not first:
                    act.wait_ge(w_used, u - 1)
                A(whi[:, q % 2, :], raw[:, q % RAW, :], ACT.Copy).then_inc(hi_done, 1)

            def his(upto):
                while hi_next[0] < min(upto, DEPTH * UNITS):
                    hi(hi_next[0], hi_next[0], first=hi_next[0] < 2)
                    hi_next[0] += 1

            def barrier(next_unit):
                his(next_unit + 2)
                nph[0] += 1
                act.drain().then_inc(act_phase, 1)
                act.wait_ge(pe_phase, nph[0])
                act.wait_ge(dve_phase, nph[0])

            def rsqrt_of(dst, src, scale):
                n = dst.shape[0]
                seq(A(dst, src, ACT.Ln, bias=eps[0:n, 0:1], scale=scale))
                return A(dst, dst, ACT.Exp, scale=-0.5)

            def exp_ln_table():
                nc.scalar.preload_act_table_set("natural_log_exp_and_others")

            def small(dst, src):
                smalls[0] += 16
                act.dma_start(dst, src).then_inc(small_in, 16)

            def mod_phase(l):
                def load(n):
                    act.dma_start(MODS["wm"][:, n % 3, :].rearrange("p (k n) -> p k n", k=KT),
                                  w_mod[l, n]).then_inc(mod_in[n % 3], 16)
                if l == 0:
                    act.wait_ge(xin, 16 * (KT + 4))
                    seq(A(csil[:, :, :], csil[:, :, :], ACT.Silu))
                for n in range(3):
                    load(n)
                for n in range(MODU):
                    act.wait_ge(mod_ps, l * MODU + n + 1)
                    A(MODS["row"][:, 512 * n:512 * n + 512], bank(n % 2)[0:2, :], ACT.Copy).then_inc(mod_row, 1)
                    if n + 3 < MODU:
                        load(n + 3)
                act.wait_ge(mod_tr, l + 1)

            def norm_phase(l, which, full):
                exp_ln_table()
                n0 = 16 * l + 8 * which
                q0 = 0 if full else CTX_LEN
                for k in range(KT):
                    if which:
                        his(u0(l, MA_OUT) + k // 2 + 3)
                        act.wait_ge(x_free, 2 + l * XPL + 2 * KT + k + 1)
                    if k >= 2:
                        act.wait_ge(sq_used, n0 + k - 1)
                    A(NRM["sq"][:, k % 2, q0:], xres[:, k, q0:], ACT.Square).then_inc(sq_done, 1)
                act.wait_ge(st_done, 2 * l + which + 1)
                rsqrt_of(NRM["r"][:, q0:], psum_pair(psum, 3)[:, q0:], 1.0 / D_MODEL).then_inc(r_done, 1)
                for k in range(KT):
                    act.wait_ge(t_done, n0 + k + 1)
                    rr = ranges(full)
                    for r0, r1 in rr:
                        ins = A(hhi[:, k, r0:r1], NRM["t"][:, k % 2, r0:r1], ACT.Identity,
                                bias=mods[:, l, 24 * which + k, cls(r0):cls(r0) + 1])
                    ins.then_inc(h_hi, 1)

            def na_inputs(l):
                small(NA["rb"][:, :], rpb[l])
                act.wait_ge(w_used, u0(l, NA_V) + 2)
                for b in range(3):
                    A(NA["vhi"][:, 2 * b:2 * b + 2, :], v_banks(psum, b),
                      ACT.Copy).then_inc(ev_a, 1)

            def na_pair(l, pr, full):
                for j in (0, 1):
                    u = u0(l, NA_QK) + 2 * pr + j
                    act.wait_ge(w_used, u + 1)
                    his(u + 3)
                    n = NAJ[l, pr, j]
                    if j:
                        act.wait_ge(ev_ps, n)
                    q0 = 0 if full or j else CTX_LEN
                    A(NA["sq"][:, q0:], psum_pair(psum, 2 + j)[:, q0:], ACT.Square).then_inc(sq2, 1)
                    act.wait_ge(ev_ps, n + 1)
                    if j:
                        act.wait_ge(ev_d, n)
                    rsqrt_of(NA["r"][:, q0:], psum_pair(psum, j)[:, q0:], 1.0 / HEAD_DIM).then_inc(rs2, 1)

            def att_act(S, l, kind, heads, scale):
                steps = [st for h in heads for st in PLAN[l, kind, h]]

                def exp_of(s, b, blk, qt, nk):
                    act.wait_ge(s_nmx, s + 1)
                    if s >= 2:
                        act.wait_ge(t_ps, s - 1)
                        act.wait_ge(s_rs, s - 1)
                    sc = psum_pair(psum, s % 2)
                    st = stat[:, s % 2, :]
                    pb = S["p"][:, s % 2, :]
                    if kind == "na" and blk:
                        A(pb[:, 0:CTX_LEN], sc[:, 0:CTX_LEN], ACT.Exp, bias=st[:, 2:3], accum_out=st[:, 4:5])
                        A(pb[:, CTX_LEN:], S["s2"][:, s % 2, :], ACT.Exp, bias=st[:, 2:3],
                          accum_out=st[:, 5:6]).then_inc(s_exp, 1)
                    else:
                        A(pb[:, 0:nk * P], sc[:, 0:nk * P], ACT.Exp, bias=st[:, 2:3], scale=scale,
                          accum_out=st[:, 4:5]).then_inc(s_exp, 1)

                def hi_of(s, b, blk, qt, nk):
                    act.wait_ge(t_ps, s + 1)
                    if b >= 2:
                        act.wait_ge(pv_ps, b - 1)
                    A(S["pthi"][:, b % 2, 0:nk, P * qt:P * qt + P],
                      psum_pair(psum, 2)[:, 0:nk * P].rearrange("p (k q) -> p k q", q=P),
                      ACT.Copy).then_inc(pt_hi, 1)

                for n, st in enumerate(steps):
                    if n:
                        hi_of(*steps[n - 1])
                    exp_of(*st)
                hi_of(*steps[-1])

            def ml_act(l, full):
                rows, tm, e, va = ML["rows"], ML["tm"], ML["e"], ML["va"]
                small(ML["sel"][:, :], c_gate[:, 0:12 * P])
                small(ML["mask"][:, :], c_gate[:, 12 * P:12 * P + TOK])
                small(ML["blk"][:, :], c_rope[:, 2 * SEQ:2 * SEQ + 130])
                his(u0(l, ML_G) + 3)
                act.wait_ge(ml_d, D_(l, "gates"))
                seq(A(rows[:, 2, :], rows[:, 1, :], ACT.Abs))
                seq(A(rows[:, 2, :], rows[:, 2, :], ACT.Exp, scale=-1.0))
                A(rows[:, 2, :], rows[:, 2, :], ACT.Ln, bias=1.0).then_inc(ml_a, 1)
                for i in range(4):
                    his(u0(l, ML_QK) + i + 3)
                    act.wait_ge(ml_d, D_(l, f"cv{i}"))
                    A(ML["qk"][:, i, :], ML["qk"][:, i, :], ACT.Silu).then_inc(ml_a, 1)
                for i in range(2):
                    u = u0(l, ML_O) + i
                    his(u + 3)
                    act.wait_ge(w_used, u + 1)
                    q0 = 0 if full else CTX_LEN
                    A(ML["osig"][:, i, q0:], psum_pair(psum, 1 + i)[:, q0:], ACT.Sigmoid).then_inc(ml_a, 1)
                exp_ln_table()
                his(u0(l, ML_V) + 2)
                act.wait_ge(w_used, u0(l, ML_V) + 2)
                for i in range(3):
                    A(va[:, 2 * i:2 * i + 2, :, 0:64],
                      bank((6, 7, 0)[i]).rearrange("p (t h d) -> p t h d", t=2, h=4), ACT.Copy).then_inc(ml_a, 1)
                his(u0(l, ML_V) + 4)
                act.wait_ge(ml_d, D_(l, "rows"))
                A(ML["small"][:, 3, :], ML["small"][:, 2, :], ACT.Exp).then_inc(ml_a, 1)
                act.wait_ge(ml_t, T_(l, "tm"))
                for g in range(2):
                    v = bank(4 + g)[:, 0:432].rearrange("p (c q r) -> p c q r", c=3, q=4)
                    A(tm[:, 3 * g:3 * g + 3, 0, :], v[:, :, 0, :], ACT.Copy)
                    ins = A(tm[:, 3 * g:3 * g + 3, 1:4, :], v[:, :, 1:4, :], ACT.Exp)
                ins.then_inc(ml_a, 1)
                act.wait_ge(ml_t, T_(l, "dec"))
                A(ML["dec"][:, :, :], bank(1)[:, 0:24].rearrange("p (x c) -> p x c", x=4), ACT.Copy).then_inc(ml_a, 1)
                for i in range(3):
                    act.wait_ge(ml_t, T_(l, f"kt{i}"))
                    A(ML["kt"][:, 2 * i:2 * i + 2, :], bank((6, 7, 0)[i]).rearrange("p (t n) -> p t n", t=2),
                      ACT.Copy).then_inc(ml_a, 1)
                def weights(r):
                    h, d = r // 2, r % 2
                    act.wait_ge(ml_t, T_(l, f"cr{r}"))
                    if r >= 2:
                        act.wait_ge(ml_t, T_(l, f"in{r - 2}"))
                    elif r == 0:
                        act.wait_ge(ml_a, A_(l, "tm"))
                    for c in range(TT):
                        ins = A(e[:, d, P * c:P * c + P], psum_pair(psum, 1)[:, P * c:P * c + P], ACT.Exp,
                                bias=tm[:, c, 0, 32 * d + h:32 * d + h + 1])
                    ins.then_inc(ml_a, 1)

                weights(0)
                for r in range(8):
                    h, d = r // 2, r % 2
                    if r < 7:
                        weights(r + 1)
                    act.wait_ge(ml_t, T_(l, f"in{r}"))
                    for g in range(2):
                        ins = A(ML["hin"][:, 4 * d + h, 3 * g:3 * g + 3, :],
                                bank(4 + 2 * d + g)[:, 0:390].rearrange("p (c n) -> p c n", c=3)
                                [:, :, 65 * (h % 2):65 * (h % 2) + 65], ACT.Copy)
                    ins.then_inc(ml_a, 1)
                act.wait_ge(ml_d, D_(l, "hsum"))
                sq = e[:, :, :].rearrange("p a t -> p (a t)").rearrange("p (h c n) -> p h c n", h=4, c=TT)
                A(sq, ML["hin"][:, 0:4, :, 0:64], ACT.Square).then_inc(ml_a, 1)
                act.wait_ge(ml_d, D_(l, "ssq"))
                rsqrt_of(ML["ssq"][:, :, :], ML["ssq"][:, :, :], 1.0 / HEAD_DIM).then_inc(ml_a, 1)

            def ma_act(l, full):
                small(MA["rope"][:, :, :], c_rope[:, 0:2 * SEQ].rearrange("p (a t) -> p a t", a=2))
                for n, (off, cnt, div) in enumerate(((MA_CQ, 3, Q_LORA), (MA_CKV, 2, KV_LORA))):
                    q0 = 0 if full or n else CTX_LEN
                    for i in range(cnt):
                        u = u0(l, off) + i
                        his(u + 3)
                        act.wait_ge(w_used, u + 1)
                        if n or i:
                            act.wait_ge(ma_t, MT_(l, "c%d" % (3 * n + i - 1)))
                        A(MA["sqq"][:, q0:], psum_pair(psum, i)[:, q0:], ACT.Square).then_inc(ma_a, 1)
                    act.wait_ge(ma_t, MT_(l, "c%d" % (3 * n + cnt - 1)))
                    rsqrt_of(MA["r"][:, n, q0:], psum_pair(psum, 3 - n)[:, q0:], 1.0 / div).then_inc(ma_a, 1)
                    if n == 0:
                        u = u0(l, MA_KR)
                        his(u + 3)
                        act.wait_ge(w_used, u + 1)
                        seq(A(MA["kr"][64:128, :], psum_pair(psum, 3)[64:128, :], ACT.Copy))
                        A(MA["sqk"][64:96, :], MA["kr"][64:96, :], ACT.Square).then_inc(ma_a, 1)
                his(u0(l, MA_V) + 3)
                act.wait_ge(w_used, u0(l, MA_V) + 1)
                for t in range(TT):
                    A(VHI[:, t, :], bank(t), ACT.Copy).then_inc(ma_a, 1)

            def ma_head_act(l, h, full):
                q0 = 0 if full else CTX_LEN
                u = u0(l, MA_HEAD) + h // 2
                pq, pk, sq_, sk = (0, 1, 2, 3) if h % 2 == 0 else (2, 3, 0, 1)
                his(u + 2)
                act.wait_ge(ma_t, MT_(l, f"hk{h}"))
                A(MA["sqk"][0:64, :], psum_pair(psum, pk)[0:64, :], ACT.Square).then_inc(ma_a, 1)
                if h % 2 == 0:
                    act.wait_ge(ma_t, MT_(l, f"hq{h}"))
                else:
                    act.wait_ge(w_used, u + 1)
                A(MA["sqq"][0:96, q0:], psum_pair(psum, pq)[0:96, q0:], ACT.Square).then_inc(ma_a, 1)
                act.wait_ge(ma_t, MT_(l, f"tk{h}"))
                if h % 2:
                    act.wait_ge(ma_d, MD_(l, f"dk{h - 1}"))
                rsqrt_of(MA["r"][:, 1, :], psum_pair(psum, sk), 1.0 / QK_DIM).then_inc(ma_a, 1)
                act.wait_ge(ma_t, MT_(l, f"tq{h}"))
                if h % 2:
                    act.wait_ge(ma_d, MD_(l, f"dq{h - 1}"))
                rsqrt_of(MA["r"][:, 0, q0:], psum_pair(psum, sq_)[:, q0:], 1.0 / QK_DIM).then_inc(ma_a, 1)

            def ff_act(l, full):
                q0 = 0 if full else CTX_LEN

                def silu(gj, par):
                    act.wait_ge(w_used, FFB(gj) + 2)
                    act.wait_ge(ff_free, gj + 1)
                    A(FF["sa"][:, par, q0:], psum_pair(psum, 2 * par)[:, q0:], ACT.Silu).then_inc(ff_sa, 1)

                j0 = 0
                for g, n in enumerate(FF_GROUPS):
                    b = u0(l, FF_IN[g])
                    gj = l * HG + j0
                    FFB = lambda x, b=b, gj=gj: b + 2 * (x - gj)
                    his(b + 4)
                    silu(gj, 0)
                    with act.Fori(1, n // 2) as i:
                        for jj in range(2):
                            for ab in range(2):
                                q = 2 * jj + ab
                                act.wait_ge(raw_full[(b + q) % RAW], i * 16 + 16 * ((b + q) // RAW + 1))
                                hi(i * 4 + (b + q), b + q)
                            if jj == 0:
                                silu(i * 2 + (gj - 1), 1)
                            else:
                                silu(i * 2 + gj, 0)
                    hi_next[0] = b + 2 * n
                    his(b + 2 * n + 2)
                    silu(gj + n - 1, 1)
                    his(u0(l, FF_OUT[g]) + KT + (2 if g < len(FF_GROUPS) - 1 else 0))
                    j0 += n

            for l in range(DEPTH):
                full = l < DEPTH - 1
                mod_phase(l)
                barrier(u0(l, 0))
                norm_phase(l, 0, True)
                na_inputs(l)
                barrier(u0(l, NA_QK))
                for pr in range(2):
                    na_pair(l, pr, full)
                    barrier(u0(l, NA_QK) + 2 * pr + 2)
                    att_act(NA, l, "na", (2 * pr, 2 * pr + 1), 1.0)
                    barrier(u0(l, NA_QK) + 2 * pr + 2)
                his(u0(l, ML_G))
                barrier(u0(l, ML_G))
                ml_act(l, full)
                his(u0(l, MA_CQ))
                barrier(u0(l, MA_CQ))
                ma_act(l, full)
                barrier(u0(l, MA_HEAD))
                for j in range(MLA_HEADS // 2):
                    for h in (2 * j, 2 * j + 1):
                        ma_head_act(l, h, full)
                    barrier(u0(l, MA_HEAD) + j + 1)
                    att_act(MA, l, "ma", (2 * j, 2 * j + 1), QK_DIM ** -0.5)
                    barrier(u0(l, MA_HEAD) + j + 1)
                norm_phase(l, 1, full)
                his(u0(l, FF0) + 2)
                ff_act(l, full)
                barrier(u0(l + 1, 0))

        @block.tensor
        def _(pe):
            mm = nc.tensor.matmul
            nph = [0]

            def barrier():
                nph[0] += 1
                pe.drain().then_inc(pe_phase, 1)
                pe.wait_ge(act_phase, nph[0])
                pe.wait_ge(dve_phase, nph[0])

            def mm3(dst, ah, al, bh, bl, first, last):
                mm(dst, ah, bh, start=first, stop=False)
                mm(dst, ah, bl, start=False, stop=False)
                return mm(dst, al, bh, start=False, stop=last)

            def unit(u):
                pe.wait_ge(lo_done, u + 1)
                return whi[:, u % 2, :], wlo[:, u % 2, :]

            def feature_unit(u, pair, rr, srch=None, srcl=None, m=P, nk=KT, at=0, done=True, tiles=None, last=None):
                srch, srcl = (hhi, hlo) if srch is None else (srch, srcl)
                wh, wl = whi[:, u % 2, :], wlo[:, u % 2, :]
                for r0, r1 in rr:
                    dst = psum_pair(psum, pair)[0:m, r0:r1]
                    for k in range(nk):
                        c = at + k * m
                        if tiles is not None and r0 == rr[0][0]:
                            pe.wait_ge(h_lo, tiles + k + 1)
                        if last is not None and r0 == rr[0][0] and k == nk - 1:
                            pe.wait_ge(ff_free, last)
                        ins = mm3(dst, wh[:, c:c + m], wl[:, c:c + m], srch[:, k, r0:r1], srcl[:, k, r0:r1],
                                  k == 0, k == nk - 1)
                if done:
                    ins.then_inc(w_used, 1)
                return ins

            def out_units(l, part, ubase, nk, oh, ol, rr):
                per = UW // (nk * P)
                for m in range(KT):
                    u = u0(l, ubase) + m // per
                    if m % per == 0:
                        unit(u)
                    g = l * XPL + part * KT + m
                    if g - 1 > 0:
                        pe.wait_ge(x_free, g - 1)
                    ins = feature_unit(u, m % 4, rr, oh, ol, nk=nk, at=(m % per) * nk * P, done=False)
                    ins.then_inc(w_used if m % per == per - 1 else o_ps, 1)

            def mod_phase(l):
                if l == 0:
                    pe.wait_ge(act_chain, 1)
                for n in range(MODU):
                    pe.wait_ge(mod_in[n % 3], 16 * ((l * MODU + n) // 3 + 1))
                    if n >= 2:
                        pe.wait_ge(mod_row, l * MODU + n - 1)
                    for k in range(KT):
                        ins = mm(bank(n % 2)[0:2, :], csil[:, k, :],
                                 MODS["wm"][:, n % 3, 512 * k:512 * k + 512], start=k == 0, stop=k == KT - 1)
                    ins.then_inc(mod_ps, 1)
                pe.wait_ge(mod_row, (l + 1) * MODU)
                pe.wait_ge(xin, 16 * (KT + 4))
                for j in range(48):
                    ins = nc.tensor.transpose(bank(2)[:, 2 * j:2 * j + 2], MODS["row"][0:2, P * j:P * j + P],
                                              ident[0:2, 0:2])
                ins.then_inc(mod_tr, 1)

            def norm_phase(l, which, full):
                pe.wait_ge(sq_used, 8 * (2 * l + which) + KT)
                for r0, r1 in ranges(full):
                    ins = mm(psum_pair(psum, 3)[:, r0:r1], ones, NRM["t"][:, 0, r0:r1], start=True, stop=True)
                ins.then_inc(st_done, 1)

            def na_inputs(l):
                ua, ub = u0(l, NA_V), u0(l, NA_V) + 1
                (ah, al), (bh, bl) = unit(ua), unit(ub)
                for k in range(KT):
                    pe.wait_ge(h_lo, 16 * l + k + 1)
                    wh, wl = (ah, al) if k < 4 else (bh, bl)
                    c = 256 * (k % 4)
                    for t in range(TT):
                        dst = bank(t)[:, 0:256]
                        mm(dst, hhi[:, k, P * t:P * t + P], wh[:, c:c + 256], start=k == 0, stop=False)
                        mm(dst, hlo[:, k, P * t:P * t + P], wh[:, c:c + 256], start=False, stop=False)
                        ins = mm(dst, hhi[:, k, P * t:P * t + P], wl[:, c:c + 256], start=False, stop=k == KT - 1)
                ins.then_inc(w_used, 2)
                pe.wait_ge(small_in, SMALLS["na", l])
                for g in range(16):
                    if g >= 2:
                        pe.wait_ge(bias_ev, 32 * l + 2 * (g - 1))
                    for half in (0, 64):
                        ins = mm(bank(6 + g % 2)[half:half + 64, 0:240], band[:, 60 - 4 * g:60 - 4 * g + 64],
                                 NA["rb"][:, :], start=True, stop=True)
                    ins.then_inc(bias_ps, 1)

            def na_pair(l, pr, full):
                for j in (0, 1):
                    u = u0(l, NA_QK) + 2 * pr + j
                    unit(u)
                    feature_unit(u, 2 + j, ranges(full or j))
                for j in (0, 1):
                    pe.wait_ge(sq2, NAJ[l, pr, j] + 1)
                    for r0, r1 in ranges(full or j):
                        ins = mm(psum_pair(psum, j)[:, r0:r1], ones2, NA["sq"][:, r0:r1], start=True, stop=True)
                    ins.then_inc(ev_ps, 1)

            def att_pe(S, l, kind, heads, qk_of, vt):
                steps = [(h,) + st for h in heads for st in PLAN[l, kind, h]]

                def scores(h, s, b, blk, qt, nk):
                    if s >= 2:
                        pe.wait_ge(s_exp, s - 1)
                    q0 = blk * 256 + qt * P
                    qh, ql, kh, kl = qk_of(h)
                    for r0, r1 in ([(0, CTX_LEN)] if blk == 0 else ranges(True)):
                        ins = mm3(psum_pair(psum, s % 2)[:, r0:r1], qh[:, q0:q0 + P], ql[:, q0:q0 + P],
                                  kh[:, r0:r1], kl[:, r0:r1], True, True)
                    ins.then_inc(s_ps, 1)

                def turn(h, s, b, blk, qt, nk):
                    pe.wait_ge(s_exp, s + 1)
                    if s >= 1:
                        pe.wait_ge(pt_lo, s)
                    for k in range(nk):
                        ins = nc.tensor.transpose(psum_pair(psum, 2)[:, P * k:P * k + P],
                                                  S["p"][:, s % 2, P * k:P * k + P], ident)
                    ins.then_inc(t_ps, 1)

                def inverse(h, s, b, blk, qt, nk):
                    pe.wait_ge(s_rs, s + 1)
                    if b >= 2:
                        pe.wait_ge(o_lo, b - 1)
                    mm(bank(6 + b % 2)[:, 256 + P * qt:256 + P * qt + P], ones, S["dg"][:, s % 2, :],
                       start=True, stop=True).then_inc(inv_ps, 1)

                def values(part, h, s, b, blk, qt, nk):
                    if part == 0:
                        pe.wait_ge(pt_lo, s + 1)
                    for k in (range(nk // 2), range(nk // 2, nk))[part]:
                        vh, vl = vt(h, k)
                        ins = mm3(bank(6 + b % 2)[:, 0:256], vh, vl, S["pthi"][:, b % 2, k, :],
                                  S["ptlo"][:, b % 2, k, :], k == 0, k == nk - 1)
                    if part:
                        ins.then_inc(pv_ps, 1)

                N = len(steps)
                for n in range(N + 3):
                    if n < N:
                        scores(*steps[n])
                    if 1 <= n < N + 1:
                        turn(*steps[n - 1])
                    if n >= 3 and steps[n - 3][4] == 1:
                        values(1, *steps[n - 3])
                    if 2 <= n < N + 2:
                        inverse(*steps[n - 2])
                        if steps[n - 2][4] == 1:
                            values(0, *steps[n - 2])

            def ml_pe(l, full):
                rows, tm, e, va, sel, qk = ML["rows"], ML["tm"], ML["e"], ML["va"], ML["sel"], ML["qk"]
                for i in range(7):
                    u = u0(l, ML_G) + i
                    unit(u)
                    if i == 4:
                        pe.wait_ge(ml_d, D_(l, "gates"))
                    elif i > 4:
                        pe.wait_ge(ml_d, D_(l, f"cv{i - 5}"))
                    feature_unit(u, i % 4, ranges(full or i < 5))
                ua = u0(l, ML_V)
                (ah, al), (bh, bl) = unit(ua), unit(ua + 1)
                for t in range(TT):
                    if t % 2 == 0:
                        pe.wait_ge(ml_d, D_(l, "cv2" if t < 4 else "cv3"))
                    dst = bank((6, 7, 0)[t // 2])[:, 256 * (t % 2):256 * (t % 2) + 256]
                    for k in range(KT):
                        wh, wl = (ah, al) if k < 4 else (bh, bl)
                        c = 256 * (k % 4)
                        mm(dst, hhi[:, k, P * t:P * t + P], wh[:, c:c + 256], start=k == 0, stop=False)
                        mm(dst, hlo[:, k, P * t:P * t + P], wh[:, c:c + 256], start=False, stop=False)
                        ins = mm(dst, hhi[:, k, P * t:P * t + P], wl[:, c:c + 256], start=False, stop=k == KT - 1)
                ins.then_inc(w_used, 2)
                pe.wait_ge(ml_d, D_(l, "rows"))
                pe.wait_ge(ml_a, A_(l, "o1"))
                for c in range(TT):
                    for q, row in enumerate((0, 5, 4, 1)):
                        o = 144 * (c % 3) + 36 * q
                        ins = nc.tensor.transpose(bank(4 + c // 3)[:, o:o + 36], rows[:, row, P * c:P * c + P],
                                                  ident[0:36, 0:36])
                ins.then_inc(ml_t, 1)
                pe.wait_ge(ml_a, A_(l, "ed"))
                pe.wait_ge(small_in, SMALLS["ml", l])
                for x in range(4):
                    ins = mm(bank(1)[:, 6 * x:6 * x + 6], sel[:, 8 * P + P * x:9 * P + P * x], ML["small"][:, 3, :],
                             start=True, stop=True)
                ins.then_inc(ml_t, 1)
                pe.wait_ge(ml_d, D_(l, "k8"))
                for b in range(3):
                    pe.wait_ge(ml_a, A_(l, f"v{b}"))
                    for t in range(2):
                        for pr in range(2):
                            ins = nc.tensor.transpose(bank((6, 7, 0)[b])[:, 256 * t + P * pr:256 * t + P * pr + P],
                                                      qk[:, 2 + pr, P * (2 * b + t):P * (2 * b + t) + P], ident)
                    ins.then_inc(ml_t, 1)
                def products(h):
                    lo = 64 * (h % 2)
                    if h:
                        pe.wait_ge(ml_d, D_(l, f"p{2 * h - 1}"))
                    for c in range(TT):
                        s = slice(P * c, P * c + P)
                        ins = mm(psum_pair(psum, 0)[:, s], qk[lo:lo + 64, 2 + h // 2, s], qk[lo:lo + 64, h // 2, s],
                                 start=True, stop=True)
                    ins.then_inc(ml_t, 1)

                def exponents(r):
                    h, d = r // 2, r % 2
                    if r:
                        pe.wait_ge(ml_a, A_(l, f"e{r - 1}"))
                    for r0, r1 in ranges(True):
                        dst = psum_pair(psum, 1)[:, r0:r1]
                        x = 4 * d + h
                        mm(dst, sel[:, P * x:P * x + P], rows[:, 2, r0:r1], start=True, stop=False)
                        ins = mm(dst, identb[:, :],
                                 dirmask[:, d, :].unsqueeze(1).broadcast_to([P, (r1 - r0) // P, P]),
                                 start=False, stop=True)
                    ins.then_inc(ml_t, 1)

                pe.wait_ge(ml_a, A_(l, "kt2"))
                products(0)
                exponents(0)
                for r in range(8):
                    h, d = r // 2, r % 2
                    if r < 7:
                        exponents(r + 1)
                        if r % 2:
                            products(h + 1)
                    pe.wait_ge(ml_d, D_(l, f"p{r}"))
                    if r >= 2:
                        pe.wait_ge(ml_a, A_(l, f"h{r - 2}"))
                    for c in range(TT):
                        ins = mm(bank(4 + 2 * d + c // 3)[:, 130 * (c % 3):130 * (c % 3) + 130],
                                 e[:, d, P * c:P * c + P],
                                 va[:, c, 2 * (h // 2):2 * (h // 2) + 2, :].rearrange("p h n -> p (h n)"),
                                 start=True, stop=True)
                    ins.then_inc(ml_t, 1)
                pe.wait_ge(ml_a, A_(l, "h7"))
                for n in range(TT):
                    if n:
                        pe.wait_ge(ml_d, D_(l, f"s{n - 1}"))
                        if n >= 3:
                            pe.wait_ge(ml_d, D_(l, f"x{n - 2}"))
                        for d in range(2):
                            c = CHUNKS[d][n]
                            for pr in range(2):
                                ins = mm(bank(2 * (n % 2) + d)[:, 130 * pr:130 * pr + 130],
                                         qk[:, pr, P * c:P * c + P], ML["st"][:, n % 2, 2 * d + pr, :],
                                         start=True, stop=True)
                        ins.then_inc(ml_t, 1)
                    if n < TT - 1:
                        pe.wait_ge(ml_d, D_(l, f"kw{n}"))
                        if n >= 2:
                            pe.wait_ge(ml_d, D_(l, f"s{n - 2}"))
                        for d in range(2):
                            c = CHUNKS[d][n]
                            for pr in range(2):
                                ins = mm(bank(4 + 2 * (n % 2) + d)[:, 130 * pr:130 * pr + 130],
                                         ML["kw"][:, n % 2, d, P * pr:P * pr + P],
                                         va[:, c, 2 * pr:2 * pr + 2, :].rearrange("p h n -> p (h n)"),
                                         start=True, stop=True)
                        ins.then_inc(ml_t, 1)
                pe.wait_ge(ml_d, D_(l, "hn"))
                for c in range(TT):
                    for pr in range(2):
                        ins = nc.tensor.transpose(psum_pair(psum, pr)[:, P * c:P * c + P],
                                                  ML["kt"][:, c, P * pr:P * pr + P], ident)
                ins.then_inc(ml_t, 1)
                pe.wait_ge(ml_d, D_(l, "out"))

            def ma_pe(l, full):
                for n, (off, cnt) in enumerate(((MA_CQ, 3), (MA_CKV, 2))):
                    if n:
                        pe.wait_ge(ma_d, MD_(l, "cq"))
                    for i in range(cnt):
                        u = u0(l, off) + i
                        unit(u)
                        feature_unit(u, i, ranges(full or n))
                    for i in range(cnt):
                        pe.wait_ge(ma_a, MA_A(l, "s%d" % (3 * n + i)))
                        for r0, r1 in ranges(full or n):
                            ins = mm(psum_pair(psum, 3 - n)[:, r0:r1], ones, MA["sqq"][:, r0:r1],
                                     start=i == 0, stop=i == cnt - 1)
                        ins.then_inc(ma_t, 1)
                    if n == 0:
                        u = u0(l, MA_KR)
                        unit(u)
                        pe.wait_ge(ma_a, MA_A(l, "r0"))
                        feature_unit(u, 3, ranges(True))
                wh, wl = unit(u0(l, MA_V))
                pe.wait_ge(ma_d, MD_(l, "ck"))
                pe.wait_ge(ma_a, MA_A(l, "kr"))
                for t in range(TT):
                    for k in range(2):
                        ts = slice(P * t, P * t + P)
                        c = slice(512 * k, 512 * k + 512)
                        mm(bank(t), MA["ckhi"][:, k, ts], wh[:, c], start=k == 0, stop=False)
                        mm(bank(t), MA["cklo"][:, k, ts], wh[:, c], start=False, stop=False)
                        ins = mm(bank(t), MA["ckhi"][:, k, ts], wl[:, c], start=False, stop=k == 1)
                ins.then_inc(w_used, 1)

            def ma_head_pe(l, h, full):
                u = u0(l, MA_HEAD) + h // 2
                at = 512 * (h % 2)
                pq, pk, sq_, sk = (0, 1, 2, 3) if h % 2 == 0 else (2, 3, 0, 1)
                unit(u)
                if h % 2:
                    pe.wait_ge(ma_a, MA_A(l, f"rk{h - 1}"))
                feature_unit(u, pk, ranges(True), MA["ckhi"], MA["cklo"], m=64, nk=2, at=at + 384,
                             done=False).then_inc(ma_t, 1)
                if h % 2:
                    pe.wait_ge(ma_a, MA_A(l, f"rq{h - 1}"))
                feature_unit(u, pq, ranges(full), MA["cqhi"], MA["cqlo"], nk=3, at=at,
                             done=False).then_inc(w_used if h % 2 else ma_t, 1)
                pe.wait_ge(ma_a, MA_A(l, f"ak{h}"))
                if h % 2:
                    pe.wait_ge(ma_d, MD_(l, f"dk{h - 1}"))
                for r0, r1 in ranges(True):
                    ins = mm(psum_pair(psum, sk)[:, r0:r1], ones[0:96, :], MA["sqk"][0:96, r0:r1], start=True, stop=True)
                ins.then_inc(ma_t, 1)
                pe.wait_ge(ma_a, MA_A(l, f"aq{h}"))
                if h % 2:
                    pe.wait_ge(ma_d, MD_(l, f"dq{h - 1}"))
                for r0, r1 in ranges(full):
                    ins = mm(psum_pair(psum, sq_)[:, r0:r1], ones[0:96, :], MA["sqq"][0:96, r0:r1], start=True, stop=True)
                ins.then_inc(ma_t, 1)

            def ff_pe(l, full):
                rr = ranges(full)
                j0 = 0
                for g, n in enumerate(FF_GROUPS):
                    b, bo = u0(l, FF_IN[g]), u0(l, FF_OUT[g])
                    gj, gx = l * HG + j0, l * XPL + (3 + g) * KT
                    pe.wait_ge(x_free, gx + 2)
                    with pe.Fori(0, n // 2) as i:
                        for jj in range(2):
                            pe.wait_ge(ff_free, i * 2 + (gj + jj + 1))
                            for ab in range(2):
                                q = 2 * jj + ab
                                pe.wait_ge(lo_done, i * 4 + (b + q + 1))
                                feature_unit(b + q, q, rr, tiles=16 * l + KT if g == q == 0 else None)
                    pe.wait_ge(ff_free, gj + n + 1)
                    with pe.Fori(0, KT // 2) as i:
                        for mj in range(2):
                            pe.wait_ge(lo_done, i * 2 + (bo + mj + 1))
                            pe.wait_ge(x_free, i * 2 + (gx + mj + 1))
                            feature_unit(bo + mj, mj, rr, FF["uhi"], FF["ulo"], nk=n,
                                         last=gj + n + 2 if mj == 0 else None)
                    j0 += n

            for l in range(DEPTH):
                full = l < DEPTH - 1
                mod_phase(l)
                barrier()
                norm_phase(l, 0, True)
                na_inputs(l)
                barrier()
                for pr in range(2):
                    na_pair(l, pr, full)
                    barrier()
                    att_pe(NA, l, "na", (2 * pr, 2 * pr + 1),
                           lambda h: (NA["qhi"][:, h % 2, :], NA["qlo"][:, h % 2, :], NA["khi"], NA["klo"]),
                           lambda h, k: (NA["vhi"][:, k, P * pr:P * pr + P], NA["vlo"][:, k, P * pr:P * pr + P]))
                    barrier()
                out_units(l, 0, NA_OUT, 2, NA["ohi"], NA["olo"], ranges(full))
                barrier()
                ml_pe(l, full)
                out_units(l, 1, ML_OUT, 2, ML["ohi"], ML["olo"], ranges(full))
                barrier()
                ma_pe(l, full)
                barrier()
                for j in range(MLA_HEADS // 2):
                    for h in (2 * j, 2 * j + 1):
                        ma_head_pe(l, h, full)
                    barrier()
                    att_pe(MA, l, "ma", (2 * j, 2 * j + 1),
                           lambda h: (MA[x][0:96, h % 2, :] for x in ("qhi", "qlo", "khi", "klo")),
                           lambda h, k: (VHI[:, k, P * j:P * j + P], VLO[:, k, P * j:P * j + P]))
                    barrier()
                out_units(l, 2, MA_OUT, 4, hhi, hlo, ranges(full))
                norm_phase(l, 1, full)
                ff_pe(l, full)
                barrier()

        @block.vector
        def _(dve):
            V = nc.vector
            chain, nph = [0], [0]

            def seq(ins):
                chain[0] += 1
                ins.then_inc(dve_chain, 1)
                dve.wait_ge(dve_chain, chain[0])

            def barrier():
                nph[0] += 1
                dve.drain().then_inc(dve_phase, 1)
                dve.wait_ge(pe_phase, nph[0])
                dve.wait_ge(act_phase, nph[0])

            def split(hi, lo, src):
                seq(V.tensor_copy(hi, src))
                return V.tensor_tensor(lo, src, hi, ALU.subtract)

            def mod_phase(l):
                if l == 0:
                    dve.wait_ge(xin, 16 * (KT + 4))
                    V.tensor_copy(identb[:, :], ident)
                    V.tensor_copy(dirmask[:, :, :], dirm[:, :].rearrange("p (d s) -> p d s", d=2))
                    seq(V.tensor_scalar(lc[:, :, C_NAQ:C_NAQ + 2], lc[:, :, C_NAQ:C_NAQ + 2],
                                        HEAD_DIM ** -0.5, None, ALU.mult))
                dve.wait_ge(mod_tr, l + 1)
                for c in range(2):
                    seq(V.tensor_tensor(mods[:, l, :, c], bank(2)[:, c:96:2], lc[:, l, C_BMOD:C_BMOD + 48], ALU.add))
                for w in range(2):
                    for c in range(2):
                        ins = V.scalar_tensor_tensor(amix[:, l, w, :, c], mods[:, l, 24 * w + 8:24 * w + 16, c], 1.0,
                                                     lc[:, l, C_GMIX + 8 * w:C_GMIX + 8 * w + 8], ALU.add, ALU.mult)
                seq(ins)

            def add_square(l, which, full, k):
                n0, q0 = 16 * l + 8 * which, 0 if full else CTX_LEN
                acc = NRM["t"][:, 0, q0:]
                dve.wait_ge(sq_done, n0 + k + 1)
                if k:
                    dve.wait_ge(sq_used, n0 + k)
                    V.tensor_tensor(acc, acc, NRM["sq"][:, k % 2, q0:], ALU.add).then_inc(sq_used, 1)
                else:
                    V.tensor_copy(acc, NRM["sq"][:, 0, q0:]).then_inc(sq_used, 1)

            def norm_phase(l, which, full):
                n0 = 16 * l + 8 * which
                rr = ranges(full)
                if which:
                    add_square(l, which, full, KT - 1)
                else:
                    for k in range(KT):
                        add_square(l, which, full, k)
                dve.wait_ge(r_done, 2 * l + which + 1)

                def lower(k):
                    dve.wait_ge(h_hi, n0 + k + 1)
                    for r0, r1 in rr:
                        ins = V.scalar_tensor_tensor(hlo[:, k, r0:r1], NRM["t"][:, k % 2, r0:r1],
                                                     mods[:, l, 24 * which + k, cls(r0):cls(r0) + 1],
                                                     hhi[:, k, r0:r1], ALU.add, ALU.subtract)
                    ins.then_inc(h_lo, 1)
                for k in range(KT):
                    if k >= 2:
                        dve.wait_ge(h_lo, n0 + k - 1)
                    for r0, r1 in rr:
                        ins = V.scalar_tensor_tensor(NRM["t"][:, k % 2, r0:r1], xres[:, k, r0:r1],
                                                     amix[:, l, which, k, cls(r0):cls(r0) + 1],
                                                     NRM["r"][:, r0:r1], ALU.mult, ALU.mult)
                    ins.then_inc(t_done, 1)
                    if k:
                        lower(k - 1)
                lower(KT - 1)

            def out_add(l, part, ubase, nk, full):
                per = UW // (nk * P)
                for m in range(KT):
                    if m % per == per - 1:
                        dve.wait_ge(w_used, u0(l, ubase) + m // per + 1)
                    else:
                        dve.wait_ge(o_ps, OPS(l, part) + m - m // per)
                    for r0, r1 in ranges(full):
                        ins = V.scalar_tensor_tensor(xres[:, m, r0:r1], psum_pair(psum, m % 4)[:, r0:r1],
                                                     mods[:, l, 16 + m, cls(r0):cls(r0) + 1],
                                                     xres[:, m, r0:r1], ALU.mult, ALU.add)
                    ins.then_inc(x_free, 1)
                    if part == 2 and m:
                        add_square(l, 1, full, m - 1)

            def na_inputs(l):
                for b in range(3):
                    dve.wait_ge(ev_a, 3 * l + b + 1)
                    V.tensor_tensor(NA["vlo"][:, 2 * b:2 * b + 2, :], v_banks(psum, b),
                                    NA["vhi"][:, 2 * b:2 * b + 2, :], ALU.subtract)
                for g in range(16):
                    dve.wait_ge(bias_ps, 16 * l + g + 1)
                    for half in range(2):
                        rs = slice(64 * half, 64 * half + 64)
                        src = bank(6 + g % 2)[rs, 0:240].rearrange("p (i h r) -> p h r i", i=4, h=NA_HEADS)
                        m = colmask[rs, 4 * g:4 * g + 4].unsqueeze(1).unsqueeze(1).broadcast_to([64, NA_HEADS, NDR, 4])
                        ins = V.tensor_tensor(NA["bias"][rs, :, half:half + NDR, 4 * g:4 * g + 4], src, m, ALU.add)
                        ins.then_inc(bias_ev, 1)

            def na_pair(l, pr, full):
                for j in (0, 1):
                    n = NAJ[l, pr, j]
                    dve.wait_ge(rs2, n + 1)
                    q0 = 0 if full or j else CTX_LEN
                    src = psum_pair(psum, 2 + j)[:, q0:]
                    for a in range(2 if j == 0 else 1):
                        g = C_NAK if j else C_NAQ + a
                        seq(V.scalar_tensor_tensor(NA["t"][:, q0:], src, lc[:, l, g:g + 1], NA["r"][:, q0:], ALU.mult, ALU.mult))
                        hi, lo = (NA["khi"], NA["klo"]) if j else (NA["qhi"][:, a, :], NA["qlo"][:, a, :])
                        ins = split(hi[:, q0:], lo[:, q0:], NA["t"][:, q0:])
                        if a == 0 and j == 0:
                            seq(ins)
                    ins.then_inc(ev_d, 1)
                dve.wait_ge(ev_d, NAJ[l, pr, 1] + 1)

            def att_dve(S, l, kind, heads, scale, dst):
                steps = [(h,) + st for h in heads for st in PLAN[l, kind, h]]

                def max_of(h, s, b, blk, qt, nk):
                    dve.wait_ge(s_ps, s + 1)
                    if s >= 2:
                        dve.wait_ge(s_exp, s - 1)
                    sc = psum_pair(psum, s % 2)
                    st = stat[:, s % 2, :]
                    if kind == "na" and blk:
                        t = (blk - 1) * 2 + qt
                        win = S["bias"][:, h, NA_WIN_R - 1 - 2 * t:2 * NA_WIN_R - 1 - 2 * t, :].rearrange("p r c -> p (r c)")
                        V.tensor_tensor_reduce(S["s2"][:, s % 2, :], sc[:, CTX_LEN:], win, 1.0, NEG,
                                               ALU.add, ALU.max, st[:, 0:1])
                        seq(V.tensor_reduce(st[:, 1:2], sc[:, 0:CTX_LEN], AX.X, ALU.max))
                        V.tensor_scalar(st[:, 2:3], st[:, 0:1], st[:, 1:2], -1.0, ALU.max, ALU.mult).then_inc(s_nmx, 1)
                    else:
                        seq(V.tensor_reduce(st[:, 0:1], sc[:, 0:nk * P], AX.X, ALU.max))
                        V.tensor_scalar(st[:, 2:3], st[:, 0:1], -scale, None, ALU.mult).then_inc(s_nmx, 1)

                def rs_of(h, s, b, blk, qt, nk):
                    dve.wait_ge(s_exp, s + 1)
                    if s >= 2:
                        dve.wait_ge(inv_ps, s - 1)
                    st = stat[:, s % 2, :]
                    if kind == "na" and blk:
                        seq(V.tensor_tensor(st[:, 4:5], st[:, 4:5], st[:, 5:6], ALU.add))
                    seq(V.reciprocal(st[:, 6:7], st[:, 4:5]))
                    V.tensor_scalar(S["dg"][:, s % 2, :], ident, st[:, 6:7], None, ALU.mult).then_inc(s_rs, 1)

                def lo_of(h, s, b, blk, qt, nk):
                    dve.wait_ge(pt_hi, s + 1)
                    V.tensor_tensor(S["ptlo"][:, b % 2, 0:nk, P * qt:P * qt + P],
                                    psum_pair(psum, 2)[:, 0:nk * P].rearrange("p (k q) -> p k q", q=P),
                                    S["pthi"][:, b % 2, 0:nk, P * qt:P * qt + P], ALU.subtract).then_inc(pt_lo, 1)

                def o_of(h, s, b, blk, qt, nk):
                    dve.wait_ge(pv_ps, b + 1)
                    rows, cols_ = slice(64 * (h % 2), 64 * (h % 2) + 64), slice(256 * blk, 256 * blk + 256)
                    dst_hi, dst_lo = dst(h)
                    of = S["of"][rows, :]
                    seq(V.tensor_copy(of, bank(6 + b % 2)[rows, 256:512]))
                    seq(V.tensor_tensor(of, bank(6 + b % 2)[rows, 0:256], of, ALU.mult))
                    split(dst_hi[rows, cols_], dst_lo[rows, cols_], of).then_inc(o_lo, 1)
                    dve.wait_ge(o_lo, b + 1)

                N = len(steps)
                for n in range(N + 4):
                    if n < N:
                        max_of(*steps[n])
                    if 1 <= n < N + 1:
                        rs_of(*steps[n - 1])
                        lo_of(*steps[n - 1])
                    if n >= 4 and steps[n - 4][4] == 1:
                        o_of(*steps[n - 4])

            def ml_dve(l, full):
                rows, tm, e, va, qk, hin = ML["rows"], ML["tm"], ML["e"], ML["va"], ML["qk"], ML["hin"]
                small = ML["small"]
                V.memset(rows[:, 3:5, :], 0.0)
                V.memset(small[:, :, :], 0.0)
                V.memset(va[:, :, :, 64:65], 1.0)
                dve.wait_ge(small_in, SMALLS["ml", l])
                dve.wait_ge(w_used, u0(l, ML_G) + 1)
                V.tensor_scalar(rows[:, 0, :], psum_pair(psum, 0)[0:36, :], lc[0:36, l, C_GM:C_GM + 1],
                                lc[0:36, l, C_GI:C_GI + 1], ALU.mult, ALU.add)
                V.tensor_scalar(rows[:, 1, :], psum_pair(psum, 0)[64:100, :], lc[0:36, l, C_GM:C_GM + 1],
                                lc[0:36, l, C_GF:C_GF + 1], ALU.mult, ALU.add).then_inc(ml_d, 1)

                def conv(i):
                    dve.wait_ge(w_used, u0(l, ML_QK) + i + 1)
                    src, y = psum_pair(psum, (i + 1) % 4), qk[:, i, :]
                    w = [lc[:, l, C_CONV + 4 * i + j:C_CONV + 4 * i + j + 1] for j in range(4)]
                    seq(V.tensor_scalar(y, src, w[1], w[3], ALU.mult, ALU.add))
                    for r0, r1 in ranges(True):
                        V.scalar_tensor_tensor(y[:, r0 + 1:r1], src[:, r0:r1 - 1], w[0], y[:, r0 + 1:r1],
                                               ALU.mult, ALU.add)
                    seq(V.drain())
                    for r0, r1 in ranges(True):
                        ins = V.scalar_tensor_tensor(y[:, r0:r1 - 1], src[:, r0 + 1:r1], w[2], y[:, r0:r1 - 1],
                                                     ALU.mult, ALU.add)
                    ins.then_inc(ml_d, 1)

                conv(0)
                dve.wait_ge(ml_a, A_(l, "sp"))
                seq(V.scalar_tensor_tensor(rows[:, 1, :], rows[:, 1, :], 0.0, rows[:, 2, :], ALU.min, ALU.subtract))
                def scan(d, out_row, in0, in1, op0, op1, r0, r1, init):
                    rs = slice(32 * d, 32 * d + 4)
                    step = -1 if d else 1
                    f = lambda x: x[rs, r0:r1][:, ::step]
                    return V.tensor_tensor_scan(f(rows[:, out_row, :]), f(in0), f(in1), init, op0, op1)
                lf, gi, b, m = (rows[:, j, :] for j in (1, 0, 3, 4))
                for d in range(2):
                    scan(d, 3, ML["mask"], lf, ALU.mult, ALU.add, 0, TOK, 0.0)
                scan(0, 4, lf, gi, ALU.add, ALU.max, 0, TOK, 0.0)
                seq(scan(1, 4, lf, gi, ALU.add, ALU.max, 0, CTX_LEN, 0.0))
                seq(scan(1, 4, lf, gi, ALU.add, ALU.max, CTX_LEN, TOK, m[32:36, 0:1]))
                seq(V.tensor_tensor(rows[:, 2, :], b, m, ALU.subtract))
                seq(V.tensor_tensor(rows[:, 0, :], gi, b, ALU.subtract))
                c_, L = rows[:, 2, :], ML_CHUNK
                V.tensor_copy(small[0:4, 0, 1:TT], m[0:4, L - 1:TOK - 1:L])
                V.tensor_copy(small[32:36, 0, 0:1], m[32:36, L:L + 1])
                V.tensor_copy(small[32:36, 0, CT:TT - 1], m[32:36, CTX_LEN + L:TOK:L])
                V.tensor_copy(small[32:36, 0, TT - 1:TT], m[32:36, 0:1])
                V.tensor_copy(small[0:4, 1, :], c_[0:4, L - 1:TOK:L])
                seq(V.tensor_copy(small[32:36, 1, :], c_[32:36, 0:TOK:L]))
                bc = lambda x: x.unsqueeze(2).broadcast_to([36, TT, L])
                ch = lambda x: x.rearrange("p (c s) -> p c s", c=TT)
                V.tensor_tensor(ch(rows[:, 5, :]), ch(c_), bc(small[:, 0, :]), ALU.add)
                V.tensor_tensor(ch(rows[:, 1, :]), ch(rows[:, 0, :]), bc(small[:, 1, :]), ALU.add)
                seq(V.tensor_scalar(rows[:, 4, :], m, -1.0, None, ALU.mult))
                V.tensor_tensor(small[:, 2, :], small[:, 0, :], small[:, 1, :], ALU.add).then_inc(ml_d, 1)
                for i in range(1, 4):
                    conv(i)
                dve.wait_ge(ml_a, A_(l, "cv3"))
                V.tensor_scalar(qk[:, 2:4, :], qk[:, 2:4, :], HEAD_DIM ** -0.5, None, ALU.mult).then_inc(ml_d, 1)
                for r in range(8):
                    h, d = r // 2, r % 2
                    dve.wait_ge(ml_a, A_(l, f"e{r}"))
                    dve.wait_ge(ml_t, T_(l, f"st{r - r % 2}"))
                    V.tensor_tensor(e[:, d, :], e[:, d, :], psum_pair(psum, 0), ALU.mult).then_inc(ml_d, 1)

                def keys(n):
                    if n >= 2:
                        dve.wait_ge(ml_t, T_(l, f"u{n - 2}"))
                    for d in range(2):
                        c = CHUNKS[d][n]
                        ins = V.tensor_tensor(ML["kw"][:, n % 2, d, :].rearrange("p (h n) -> p h n", h=4),
                                              ML["kt"][:, c, :].rearrange("p (h n) -> p h n", h=4),
                                              tm[:, c, 3, 32 * d:32 * d + 4].unsqueeze(2).broadcast_to([P, 4, 64]),
                                              ALU.mult)
                    ins.then_inc(ml_d, 1)

                def state(n):
                    dve.wait_ge(ml_t, T_(l, f"u{n}"))
                    if n >= 2:
                        dve.wait_ge(ml_t, T_(l, f"x{n - 1}"))
                    for d in range(2):
                        c = CHUNKS[d][n]
                        um = ML["um"] if n else ML["st"][:, 1, 2 * d:2 * d + 2, :]
                        ins = V.tensor_tensor(um[:, :, :] if n else um,
                                              bank(4 + 2 * (n % 2) + d)[:, 0:260].rearrange("p (a n) -> p a n", a=2),
                                              ML["blk"][:, :].unsqueeze(1).broadcast_to([P, 2, 130]), ALU.mult)
                        if n:
                            seq(ins)
                            for pr in range(2):
                                x = 2 * d + pr
                                ins = V.scalar_tensor_tensor(ML["st"][:, (n + 1) % 2, x, :], ML["st"][:, n % 2, x, :],
                                                             ML["dec"][:, x, c:c + 1], ML["um"][:, pr, :],
                                                             ALU.mult, ALU.add)
                            if d == 0:
                                seq(ins)
                    ins.then_inc(ml_d, 1)
                    dve.wait_ge(ml_d, D_(l, f"s{n}"))

                def inter(n):
                    dve.wait_ge(ml_t, T_(l, f"x{n}"))
                    for d in range(2):
                        c = CHUNKS[d][n]
                        seq(V.tensor_tensor(ML["hs"][:, d, :, :],
                                            bank(2 * (n % 2) + d)[:, 0:260].rearrange("p (h n) -> p h n", h=4),
                                            tm[:, c, 1, 32 * d:32 * d + 4].unsqueeze(2).broadcast_to([P, 4, 65]),
                                            ALU.mult))
                        ins = V.tensor_tensor(hin[:, 4 * d:4 * d + 4, c, :], hin[:, 4 * d:4 * d + 4, c, :],
                                              ML["hs"][:, d, :, :], ALU.add)
                        if d == 0:
                            seq(ins)
                    ins.then_inc(ml_d, 1)

                dve.wait_ge(ml_a, A_(l, "h7"))
                keys(0)
                for n in range(TT):
                    if n < TT - 2:
                        keys(n + 1)
                    if n < TT - 1:
                        state(n)
                    if n:
                        inter(n)
                dve.wait_ge(ml_d, D_(l, f"x{TT - 1}"))
                den = ML["den"]
                seq(V.scalar_tensor_tensor(den[:, :, :], hin[:, :, :, 64], -1.0, hin[:, :, :, 64], ALU.mult, ALU.max))
                for d in range(2):
                    ins = V.tensor_tensor(den[:, 4 * d:4 * d + 4, :], den[:, 4 * d:4 * d + 4, :],
                                          tm[:, :, 2, 32 * d:32 * d + 4].rearrange("p c h -> p h c"), ALU.max)
                seq(ins)
                seq(V.reciprocal(den[:, :, :], den[:, :, :]))
                seq(V.tensor_tensor(hin[:, :, :, 0:64], hin[:, :, :, 0:64],
                                    den[:, :, :].unsqueeze(3).broadcast_to([P, 8, TT, 64]), ALU.mult))
                V.tensor_tensor(hin[:, 0:4, :, 0:64], hin[:, 0:4, :, 0:64], hin[:, 4:8, :, 0:64], ALU.add)\
                    .then_inc(ml_d, 1)
                dve.wait_ge(ml_a, A_(l, "sq"))
                sq = e[:, :, :].rearrange("p a t -> p (a t)").rearrange("p (h c n) -> p h c n", h=4, c=TT)
                V.tensor_reduce(ML["ssq"][:, :, :], sq, AX.X, ALU.add).then_inc(ml_d, 1)
                dve.wait_ge(ml_a, A_(l, "rstd"))
                V.tensor_tensor(ML["kt"][:, :, :].rearrange("p c (h n) -> p h c n", h=4), hin[:, 0:4, :, 0:64],
                                ML["ssq"][:, :, :].unsqueeze(3).broadcast_to([P, 4, TT, 64]), ALU.mult).then_inc(ml_d, 1)
                dve.wait_ge(ml_t, T_(l, "ht"))
                for pr in range(2):
                    q0 = 0 if full else CTX_LEN
                    seq(V.scalar_tensor_tensor(e[:, pr, q0:], psum_pair(psum, pr)[:, q0:], lc[:, l, C_HG + pr:C_HG + pr + 1],
                                               ML["osig"][:, pr, q0:], ALU.mult, ALU.mult))
                    ins = split(ML["ohi"][:, pr, q0:], ML["olo"][:, pr, q0:], e[:, pr, q0:])
                ins.then_inc(ml_d, 1)

            def ma_dve(l, full):
                for n, (cnt, col, hi, lo) in enumerate(((3, C_CQ, MA["cqhi"], MA["cqlo"]), (2, C_CKV, MA["ckhi"], MA["cklo"]))):
                    dve.wait_ge(ma_a, MA_A(l, f"r{n}"))
                    q0 = 0 if full or n else CTX_LEN
                    for i in range(cnt):
                        seq(V.scalar_tensor_tensor(MA["t"][:, q0:], psum_pair(psum, i)[:, q0:], lc[:, l, col + i:col + i + 1],
                                                   MA["r"][:, n, q0:], ALU.mult, ALU.mult))
                        ins = split(hi[:, i, q0:], lo[:, i, q0:], MA["t"][:, q0:])
                        if i < cnt - 1:
                            seq(ins)
                    ins.then_inc(ma_d, 1)
                    dve.wait_ge(ma_d, MD_(l, ("cq", "ck")[n]))
                dve.wait_ge(small_in, SMALLS["ma", l])
                kr, t = MA["kr"], MA["t"]
                dve.wait_ge(ma_a, MA_A(l, "kr"))
                seq(V.tensor_scalar(t[64:128, :], kr[64:128, :], lc[64:128, l, C_MK:C_MK + 1], None, ALU.mult))
                rotate(t)
                V.tensor_copy(kr[64:96, :], t[64:96, :])
                for t in range(TT):
                    dve.wait_ge(ma_a, MA_A(l, f"v{t}"))
                    V.tensor_tensor(VLO[:, t, :], bank(t), VHI[:, t, :], ALU.subtract)

            def rotate(buf):
                X = slice(CTX_LEN, TOK)
                V.tensor_tensor(MA["p"][64:96, 0, 0:SEQ], buf[96:128, X], MA["rope"][96:128, 1, :], ALU.mult)
                seq(V.tensor_tensor(MA["p"][64:96, 1, 0:SEQ], buf[64:96, X], MA["rope"][64:96, 0, :], ALU.mult))
                seq(V.tensor_tensor(buf[64:96, X], MA["p"][64:96, 0, 0:SEQ], MA["p"][64:96, 1, 0:SEQ], ALU.add))

            def ma_head_dve(l, h, full):
                q0 = 0 if full else CTX_LEN
                pq, pk = (0, 1) if h % 2 == 0 else (2, 3)
                for what, buf, q, ri in (("rk", MA["t"], 0, 1), ("rq", MA["t2"], q0, 0)):
                    dve.wait_ge(ma_a, MA_A(l, f"{what}{h}"))
                    g = C_MK if ri else C_MQ
                    if ri:
                        V.scalar_tensor_tensor(buf[0:64, :], psum_pair(psum, pk)[0:64, :], lc[0:64, l, g:g + 1],
                                               MA["r"][0:64, 1, :], ALU.mult, ALU.mult)
                        seq(V.tensor_tensor(buf[64:96, :], MA["kr"][64:96, :], MA["r"][64:96, 1, :], ALU.mult))
                    else:
                        seq(V.scalar_tensor_tensor(buf[:, q:], psum_pair(psum, pq)[:, q:], lc[:, l, g:g + 1],
                                                   MA["r"][:, 0, q:], ALU.mult, ALU.mult))
                        rotate(buf)
                    hi, lo = (MA["khi"][:, h % 2], MA["klo"][:, h % 2]) if ri else (MA["qhi"][:, h % 2], MA["qlo"][:, h % 2])
                    split(hi[0:96, q:], lo[0:96, q:], buf[0:96, q:]).then_inc(ma_d, 1)
                    dve.wait_ge(ma_d, MD_(l, ("dq", "dk")[ri] + str(h)))

            def ff_dve(l, full):
                q0 = 0 if full else CTX_LEN
                j0 = 0
                for g, n in enumerate(FF_GROUPS):
                    b, bo = u0(l, FF_IN[g]), u0(l, FF_OUT[g])
                    gj, gx = l * HG + j0, l * XPL + (3 + g) * KT
                    with dve.Fori(0, n // 2) as i:
                        for jj in range(2):
                            dve.wait_ge(ff_sa, i * 2 + (gj + jj + 1))
                            V.tensor_tensor(FF["uf"][:, jj, q0:], FF["sa"][:, jj, q0:],
                                            psum_pair(psum, 2 * jj + 1)[:, q0:], ALU.mult).then_inc(ff_uf, 1)
                            dve.wait_ge(ff_uf, i * 2 + (gj + jj + 1))
                            V.tensor_copy(FF["uhi"][:, bass.ds(i * 2 + jj, 1), q0:].rearrange("p o t -> p (o t)"),
                                          FF["uf"][:, jj, q0:]).then_inc(ff_uhi, 1)
                            dve.wait_ge(ff_uhi, i * 2 + (gj + jj + 1))
                            V.tensor_tensor(FF["ulo"][:, bass.ds(i * 2 + jj, 1), q0:].rearrange("p o t -> p (o t)"),
                                            FF["uf"][:, jj, q0:],
                                            FF["uhi"][:, bass.ds(i * 2 + jj, 1), q0:].rearrange("p o t -> p (o t)"),
                                            ALU.subtract).then_inc(ff_free, 1)
                    with dve.Fori(0, KT // 2) as i:
                        for mj in range(2):
                            dve.wait_ge(w_used, i * 2 + (bo + mj + 1))
                            for r0, r1 in ranges(full):
                                xm = xres[:, bass.ds(i * 2 + mj, 1), r0:r1].rearrange("p o t -> p (o t)")
                                gate = mods[:, l, bass.ds(i * 2 + (40 + mj), 1), cls(r0):cls(r0) + 1]\
                                    .rearrange("p o t -> p (o t)")
                                ins = V.scalar_tensor_tensor(xm, psum_pair(psum, mj)[:, r0:r1], gate, xm,
                                                             ALU.mult, ALU.add)
                            ins.then_inc(x_free, 1)
                    j0 += n

            V.memset(eps[:, :], EPS).then_inc(ff_free, 2)
            V.memset(stat[:, :, :], 0.0).then_inc(x_free, 2)
            for l in range(DEPTH):
                full = l < DEPTH - 1
                mod_phase(l)
                barrier()
                norm_phase(l, 0, True)
                seq(V.drain())
                na_inputs(l)
                barrier()
                for pr in range(2):
                    na_pair(l, pr, full)
                    barrier()
                    att_dve(NA, l, "na", (2 * pr, 2 * pr + 1), 1.0, lambda h: (NA["ohi"][:, pr, :], NA["olo"][:, pr, :]))
                    barrier()
                out_add(l, 0, NA_OUT, 2, full)
                barrier()
                ml_dve(l, full)
                out_add(l, 1, ML_OUT, 2, full)
                barrier()
                ma_dve(l, full)
                barrier()
                for j in range(MLA_HEADS // 2):
                    for h in (2 * j, 2 * j + 1):
                        ma_head_dve(l, h, full)
                    barrier()
                    att_dve(MA, l, "ma", (2 * j, 2 * j + 1), QK_DIM ** -0.5, lambda h: (hhi[:, h // 2, :], hlo[:, h // 2, :]))
                    barrier()
                out_add(l, 2, MA_OUT, 4, full)
                norm_phase(l, 1, full)
                seq(V.drain())
                ff_dve(l, full)
                barrier()


def weight_units(w_in, w_uq, w_ukv, w_out, w_ffn_in, w_ffn_out):
    na, ml = NA_HEADS * HEAD_DIM, ML_HEADS * HEAD_DIM
    o_v, o_ml = 2 * na, 3 * na
    o_g = o_ml + 4 * ml
    o_cq = o_g + NG
    o_ckv, o_kr = o_cq + Q_LORA, o_cq + Q_LORA + KV_LORA
    s = np.zeros((DEPTH, UNITS, P, UW), np.float32)

    def rows(w):
        return w.reshape(-1, P, w.shape[1]).transpose(1, 0, 2)

    for l in range(DEPTH):
        def put(u, *parts):
            flat = np.concatenate([x.reshape(P, -1) for x in parts], axis=1)
            s[l, u, :, :flat.shape[1]] = flat
        wi = rows(w_in[l])
        tile = lambda c: wi[:, :, c:c + P]
        for half in range(2):
            put(NA_V + half, wi[:, 4 * half:4 * half + 4, o_v:o_v + na])
            put(ML_V + half, wi[:, 4 * half:4 * half + 4, o_ml + 2 * ml:o_ml + 3 * ml])
        for pr in range(2):
            put(NA_QK + 2 * pr, tile(P * pr))
            put(NA_QK + 2 * pr + 1, tile(na + P * pr))
            put(ML_QK + pr, tile(o_ml + P * pr))
            put(ML_QK + 2 + pr, tile(o_ml + ml + P * pr))
            put(ML_O + pr, tile(o_ml + 3 * ml + P * pr))
        g = np.zeros((P, KT, P), np.float32)
        for at, n in ((0, 0), (64, 1), (32, 2), (96, 3)):
            g[:, :, at:at + ML_HEADS] = wi[:, :, o_g + ML_HEADS * n:o_g + ML_HEADS * (n + 1)]
        put(ML_G, g)
        for i in range(3):
            put(MA_CQ + i, tile(o_cq + P * i))
        for i in range(2):
            put(MA_CKV + i, tile(o_ckv + P * i))
        r = np.zeros((P, KT, P), np.float32)
        h2 = ROPE // 2
        r[:, :, NOPE:QK_DIM] = wi[:, :, o_kr:o_kr + ROPE]
        r[:, :, QK_DIM:QK_DIM + h2] = wi[:, :, o_kr + h2:o_kr + ROPE]
        r[:, :, QK_DIM + h2:] = wi[:, :, o_kr:o_kr + h2]
        put(MA_KR, r)
        uq = rows(w_uq[l]).reshape(P, Q_LORA // P, MLA_HEADS, QK_DIM)
        uq = np.concatenate([uq, uq[..., NOPE + h2:], uq[..., NOPE:NOPE + h2]], axis=-1)
        ukv = rows(w_ukv[l]).reshape(P, KV_LORA // P, MLA_HEADS, NOPE + V_DIM)
        put(MA_V, ukv[..., NOPE:])
        for j in range(MLA_HEADS // 2):
            put(MA_HEAD + j, uq[:, :, 2 * j], ukv[:, :, 2 * j, :NOPE], uq[:, :, 2 * j + 1], ukv[:, :, 2 * j + 1, :NOPE])
        wo = rows(w_out[l]).reshape(P, KT, KT, P)
        for j in range(2):
            put(NA_OUT + j, wo[:, 0:2, 4 * j:4 * j + 4].transpose(0, 2, 1, 3))
            put(ML_OUT + j, wo[:, 2:4, 4 * j:4 * j + 4].transpose(0, 2, 1, 3))
        for j in range(4):
            put(MA_OUT + j, wo[:, 4:8, 2 * j:2 * j + 2].transpose(0, 2, 1, 3))
        fi, fo = rows(w_ffn_in[l]), rows(w_ffn_out[l])
        j0 = 0
        for g_, n in enumerate(FF_GROUPS):
            for j in range(n):
                put(FF_IN[g_] + 2 * j, fi[:, :, P * (j0 + j):P * (j0 + j) + P])
                put(FF_IN[g_] + 2 * j + 1, fi[:, :, D_FF + P * (j0 + j):D_FF + P * (j0 + j) + P])
            for m in range(KT):
                put(FF_OUT[g_] + m, fo[:, j0:j0 + n, P * m:P * m + P])
            j0 += n
    return s.reshape(DEPTH * UNITS, P, UW)


def columns(g_mix, g_ffn, b_mod, na_qk_gain, b_gate, ml_conv_w, ml_conv_b, ml_head_gain, mla_gq, mla_gkv, mla_qk_gain):
    c = np.zeros((P, DEPTH, NCOL), np.float32)
    tiles = lambda v: v.reshape(-1, P).T
    for l in range(DEPTH):
        c[:, l, C_GMIX:C_GMIX + KT] = tiles(g_mix[l])
        c[:, l, C_GFFN:C_GFFN + KT] = tiles(g_ffn[l])
        c[:, l, C_BMOD:C_BMOD + 48] = tiles(b_mod[l])
        c[0:64, l, C_NAQ] = na_qk_gain[l, 0]
        c[64:128, l, C_NAQ + 1] = na_qk_gain[l, 0]
        c[0:64, l, C_NAK] = c[64:128, l, C_NAK] = na_qk_gain[l, 1]
        g = b_gate[l].reshape(4, ML_HEADS)
        for d in range(2):
            c[32 * d:32 * d + ML_HEADS, l, C_GI] = g[2 * d]
            c[32 * d:32 * d + ML_HEADS, l, C_GF] = g[2 * d + 1]
            c[32 * d:32 * d + ML_HEADS, l, C_GM] = 1.0
        for i in range(4):
            for j in range(3):
                c[:, l, C_CONV + 4 * i + j] = ml_conv_w[l, j, P * i:P * i + P]
            c[:, l, C_CONV + 4 * i + 3] = ml_conv_b[l, P * i:P * i + P]
        c[:, l, C_HG:C_HG + 2] = tiles(ml_head_gain[l].reshape(-1))
        c[:, l, C_CQ:C_CQ + 3] = tiles(mla_gq[l])
        c[:, l, C_CKV:C_CKV + 2] = tiles(mla_gkv[l])
        for n, col in ((0, C_MQ), (1, C_MK)):
            g = mla_qk_gain[l, n]
            h2 = ROPE // 2
            c[:, l, col] = np.concatenate([g, g[NOPE + h2:], g[NOPE:NOPE + h2]])
    return c


def tables():
    f = np.zeros((P, 3 * P + 256 + 64), np.float32)
    f[:, 0:P] = np.eye(P)
    f[:, P:2 * P] = 1.0
    for a in range(2):
        f[64 * a:64 * a + 64, 2 * P + 64 * a:2 * P + 64 * a + 64] = 1.0
    for i in range(4):
        for j in range(NDC):
            f[32 * i + j, 3 * P + 75 + i - j] = 1.0
    col = np.arange(GRID_W)
    start = np.clip(col - NA_WIN_C // 2, 0, GRID_W - NA_WIN_C)
    inside = (col[None, :] >= start[:, None]) & (col[None, :] < start[:, None] + NA_WIN_C)
    f[:, 3 * P + 256:] = np.tile(np.where(inside, 0.0, NEG), (2, 1))
    rope = np.zeros((P, 2 * SEQ + 130), np.float32)
    nf = ROPE // 4
    inv = (np.float32(ROPE_BASE) ** (-np.arange(nf, dtype=np.float32) / np.float32(nf))).astype(np.float32)
    t = np.arange(SEQ)
    ang = np.concatenate([(t // GRID_W).astype(np.float32)[:, None] * inv, (t % GRID_W).astype(np.float32)[:, None] * inv], -1)
    cos, sin = np.cos(ang).T, np.sin(ang).T
    rope[64:80, 0:SEQ] = rope[80:96, 0:SEQ] = cos
    rope[96:112, SEQ:2 * SEQ] = -sin
    rope[112:128, SEQ:2 * SEQ] = sin
    rope[0:64, 2 * SEQ:2 * SEQ + 65] = 1.0
    rope[64:128, 2 * SEQ + 65:] = 1.0
    gate = np.zeros((36, 12 * P + TOK), np.float32)
    for d in range(2):
        for h in range(ML_HEADS):
            gate[32 * d + h, P * (4 * d + h):P * (4 * d + h) + P] = 1.0
            x = 8 + 2 * d + h // 2
            gate[32 * d + h, P * x + 64 * (h % 2):P * x + 64 * (h % 2) + 64] = 1.0
    tok = np.arange(TOK)
    gate[0:4, 12 * P:] = tok % ML_CHUNK != 0
    gate[32:36, 12 * P:] = tok % ML_CHUNK != ML_CHUNK - 1
    direction = np.zeros((P, 2 * P), np.float32)
    s, q = np.meshgrid(np.arange(P), np.arange(P), indexing="ij")
    direction[:, 0:P] = np.where(s <= q, 0.0, NEG)
    direction[:, P:] = np.where(s >= q, 0.0, NEG)
    return f, rope, gate, direction


def arrays_of(x, c, ctx, c_ctx, w_mod, b_mod, g_mix, g_ffn, w_in, b_gate, na_qk_gain, na_rpb, ml_conv_w, ml_conv_b,
              ml_head_gain, mla_gq, mla_gkv, w_uq, w_ukv, mla_qk_gain, w_out, w_ffn_in, w_ffn_out):
    n = np.asarray
    fm = lambda a: n(a).T.reshape(KT, P, -1).transpose(1, 0, 2)
    f, rope, gate, direction = tables()
    rpb = np.zeros((DEPTH, 4, 32, 4, NA_HEADS * NDR), np.float32)
    for i in range(4):
        rpb[:, i, 0:NDC, i] = n(na_rpb).reshape(DEPTH, NA_HEADS * NDR, NDC).transpose(0, 2, 1)
    return {
        "x_t": np.concatenate([fm(n(ctx)[0]), fm(n(x)[0])], axis=2),
        "c_t": fm(np.stack([n(c)[0], n(c_ctx)])),
        "w_mod": n(w_mod).reshape(DEPTH, KT, P, MODU, 512).transpose(0, 3, 2, 1, 4),
        "w_stream": weight_units(n(w_in), n(w_uq), n(w_ukv), n(w_out), n(w_ffn_in), n(w_ffn_out)),
        "cols": columns(*(n(a) for a in (g_mix, g_ffn, b_mod, na_qk_gain, b_gate, ml_conv_w, ml_conv_b, ml_head_gain,
                                         mla_gq, mla_gkv, mla_qk_gain))),
        "rpb": rpb.reshape(DEPTH, P, 4 * NA_HEADS * NDR),
        "c_f32": f, "c_rope": rope, "c_gate": gate, "c_dir": direction,
    }


def kernel(**inputs):
    import concourse.bacc as bacc
    from concourse.bass_utils import run_bass_kernel_spmd

    nc = bacc.Bacc("TRN2", target_bir_lowering=False, num_devices=1)
    arrays = {k: np.ascontiguousarray(v) for k, v in arrays_of(**inputs).items()}
    aps = [nc.dram_tensor(k, v.shape, mybir.dt.from_np(v.dtype), kind="ExternalInput").ap() for k, v in arrays.items()]
    aps.append(nc.dram_tensor("out", (P, KT, SEQ), mybir.dt.float32, kind="ExternalOutput").ap())
    build(nc, *aps)
    r = run_bass_kernel_spmd(nc, [arrays], core_ids=[0])
    y = r.results[0]["out"]
    return np.ascontiguousarray(y.transpose(2, 1, 0).reshape(1, SEQ, D_MODEL))
```
